# Optimizing a Trainium2 kernel written in Bass

```python
import jax, jax.numpy as jnp
from jax import lax
import numpy as np

D_MODEL = 1024
BATCH = 1
SEQ = 256
DEPTH = 2

HEAD_DIM = 64
MIX_WIDTH = D_MODEL
FOX_HEADS = MIX_WIDTH // (2 * HEAD_DIM)
DSA_HEADS = MIX_WIDTH // (2 * HEAD_DIM)
MOBA_HEADS = MIX_WIDTH // HEAD_DIM
FOX_W = FOX_HEADS * HEAD_DIM
DSA_W = DSA_HEADS * HEAD_DIM
MOBA_W = MOBA_HEADS * HEAD_DIM
ROT_DIM = HEAD_DIM // 4
ROPE_THETA = 500000.0
Q_BLOCK = 128
IDX_HEADS = 8
IDX_DIM = 64
DSA_TOPK = 256
MOBA_BLOCK = 256
MOBA_TOPK = 3
MOBA_Q_CHUNK = 64
MEM_TOKENS = 256
MEM_HEADS = 4
MEM_HEAD_DIM = 64
MEM_W = MEM_HEADS * MEM_HEAD_DIM
D_FF = 2816
RMS_EPS = 1e-6

EVEN_SPLITS = (FOX_W, FOX_W, FOX_W, FOX_HEADS,
               DSA_W, DSA_W, DSA_W,
               IDX_HEADS * IDX_DIM, IDX_DIM, IDX_HEADS)
EVEN_IN = sum(EVEN_SPLITS)
EVEN_OFFSETS = tuple(sum(EVEN_SPLITS[:i + 1]) for i in range(len(EVEN_SPLITS) - 1))

kernel_name = 'hybrid_fox_dsa_moba_macaron'

def rms_norm(x, g):
    xf = x.astype(jnp.float32)
    y = xf * lax.rsqrt(jnp.mean(xf * xf, axis=-1, keepdims=True) + RMS_EPS)
    return (y * g.astype(jnp.float32)).astype(x.dtype)

def rope_tables(seq):
    pos = jnp.arange(seq, dtype=jnp.float32)
    inv = ROPE_THETA ** (-jnp.arange(0, ROT_DIM, 2, dtype=jnp.float32) / ROT_DIM)
    ang = pos[:, None] * inv[None, :]
    return jnp.cos(ang), jnp.sin(ang)

def partial_rope(x, cos, sin):
    half = ROT_DIM // 2
    c = cos[None, :, None, :]
    s = sin[None, :, None, :]
    x1 = x[..., :half].astype(jnp.float32)
    x2 = x[..., half:ROT_DIM].astype(jnp.float32)
    rot = jnp.concatenate([x1 * c - x2 * s, x2 * c + x1 * s], axis=-1).astype(x.dtype)
    return jnp.concatenate([rot, x[..., ROT_DIM:]], axis=-1)

def swiglu_ffn(h, g, w_in, w_out):
    a, b = jnp.split(rms_norm(h, g) @ w_in, 2, axis=-1)
    return (jax.nn.silu(a) * b) @ w_out

def forgetting_attention(q, k, v, log_f):
    B, S, H, Dh = q.shape
    nblk = S // Q_BLOCK
    scale = Dh ** -0.5
    F = jnp.cumsum(log_f, axis=1)
    Fk = F.transpose(0, 2, 1)[:, :, None, :]
    qb = jnp.moveaxis(q.reshape(B, nblk, Q_BLOCK, H, Dh), 1, 0)
    Fq = jnp.moveaxis(F.reshape(B, nblk, Q_BLOCK, H), 1, 0)
    kpos = jnp.arange(S)

    def one_block(args):
        i, q_blk, fq_blk = args
        qpos = i * Q_BLOCK + jnp.arange(Q_BLOCK)
        s = jnp.einsum('bqhd,bkhd->bhqk', q_blk, k, preferred_element_type=jnp.float32) * scale
        s = s + fq_blk.transpose(0, 2, 1)[..., None] - Fk
        s = jnp.where(kpos[None, :] <= qpos[:, None], s, -jnp.inf)
        p = jax.nn.softmax(s, axis=-1)
        return jnp.einsum('bhqk,bkhd->bqhd', p.astype(v.dtype), v)

    out = lax.map(one_block, (jnp.arange(nblk), qb, Fq))
    return jnp.moveaxis(out, 0, 1).reshape(B, S, H, Dh)

def dsa_attention(q, k, v, iq, ik, iw):
    B, S, H, Dh = q.shape
    nblk = S // Q_BLOCK
    topk = min(DSA_TOPK, S // 4)
    scale = Dh ** -0.5
    qb = jnp.moveaxis(q.reshape(B, nblk, Q_BLOCK, H, Dh), 1, 0)
    iqb = jnp.moveaxis(iq.reshape(B, nblk, Q_BLOCK, IDX_HEADS, IDX_DIM), 1, 0)
    iwb = jnp.moveaxis(iw.reshape(B, nblk, Q_BLOCK, IDX_HEADS), 1, 0)
    kpos = jnp.arange(S)
    bidx = jnp.arange(B)[:, None, None]

    def one_block(args):
        i, q_blk, iq_blk, iw_blk = args
        qpos = i * Q_BLOCK + jnp.arange(Q_BLOCK)
        dots = jnp.einsum('bqhd,bkd->bqhk', iq_blk, ik, preferred_element_type=jnp.float32) * (IDX_DIM ** -0.5)
        w = iw_blk.astype(jnp.float32) * (IDX_HEADS ** -0.5)
        score = jnp.einsum('bqh,bqhk->bqk', w, jax.nn.relu(dots))
        score = jnp.where(kpos[None, None, :] <= qpos[None, :, None], score, -jnp.inf)
        _, sel = lax.top_k(score, topk)
        valid = sel <= qpos[None, :, None]
        ks = k[bidx, sel]
        vs = v[bidx, sel]
        s = jnp.einsum('bqhd,bqkhd->bhqk', q_blk, ks, preferred_element_type=jnp.float32) * scale
        s = jnp.where(valid[:, None], s, -jnp.inf)
        p = jax.nn.softmax(s, axis=-1)
        return jnp.einsum('bhqk,bqkhd->bqhd', p.astype(vs.dtype), vs)

    out = lax.map(one_block, (jnp.arange(nblk), qb, iqb, iwb))
    return jnp.moveaxis(out, 0, 1).reshape(B, S, H, Dh)

def moba_attention(q, k, v):
    B, S, H, Dh = q.shape
    scale = Dh ** -0.5
    nb = -(-S // MOBA_BLOCK)
    pad = ((0, 0), (0, nb * MOBA_BLOCK - S), (0, 0), (0, 0))
    kp = jnp.pad(k, pad)
    vp = jnp.pad(v, pad)
    kb = kp.reshape(B, nb, MOBA_BLOCK, H, Dh).transpose(0, 1, 3, 2, 4)
    vb = vp.reshape(B, nb, MOBA_BLOCK, H, Dh).transpose(0, 1, 3, 2, 4)
    kmean = jnp.mean(kb.astype(jnp.float32), axis=3)
    n_sel = min(MOBA_TOPK, nb - 1)
    nchunk = S // MOBA_Q_CHUNK
    qc = jnp.moveaxis(q.reshape(B, nchunk, MOBA_Q_CHUNK, H, Dh), 1, 0)
    bidx = jnp.arange(B)[:, None, None, None]
    hidx = jnp.arange(H)[None, None, :, None]
    blk_ids = jnp.arange(nb)

    def one_chunk(args):
        i, q_c = args
        start = i * MOBA_Q_CHUNK
        qpos = start + jnp.arange(MOBA_Q_CHUNK)
        own = start // MOBA_BLOCK
        k_own = lax.dynamic_slice_in_dim(kp, own * MOBA_BLOCK, MOBA_BLOCK, axis=1)
        v_own = lax.dynamic_slice_in_dim(vp, own * MOBA_BLOCK, MOBA_BLOCK, axis=1)
        own_pos = own * MOBA_BLOCK + jnp.arange(MOBA_BLOCK)
        s_own = jnp.einsum('bqhd,bkhd->bhqk', q_c, k_own, preferred_element_type=jnp.float32) * scale
        s_own = jnp.where(own_pos[None, :] <= qpos[:, None], s_own, -jnp.inf)
        if n_sel == 0:
            p = jax.nn.softmax(s_own, axis=-1)
            return jnp.einsum('bhqk,bkhd->bqhd', p.astype(v_own.dtype), v_own)
        gate = jnp.einsum('bqhd,bnhd->bqhn', q_c.astype(jnp.float32), kmean)
        gate = jnp.where(blk_ids < own, gate, -jnp.inf)
        _, sel = lax.top_k(gate, n_sel)
        valid = (sel < own).transpose(0, 2, 1, 3)[..., None]
        ks = kb[bidx, sel, hidx]
        vs = vb[bidx, sel, hidx]
        s_sel = jnp.einsum('bqhd,bqhnkd->bhqnk', q_c, ks, preferred_element_type=jnp.float32) * scale
        s_sel = jnp.where(valid, s_sel, -jnp.inf).reshape(B, H, MOBA_Q_CHUNK, n_sel * MOBA_BLOCK)
        p = jax.nn.softmax(jnp.concatenate([s_sel, s_own], axis=-1), axis=-1)
        p_sel = p[..., :n_sel * MOBA_BLOCK].reshape(B, H, MOBA_Q_CHUNK, n_sel, MOBA_BLOCK)
        p_own = p[..., n_sel * MOBA_BLOCK:]
        return (jnp.einsum('bhqnk,bqhnkd->bqhd', p_sel.astype(vs.dtype), vs)
                + jnp.einsum('bhqk,bkhd->bqhd', p_own.astype(v_own.dtype), v_own))

    out = lax.map(one_chunk, (jnp.arange(nchunk), qc))
    return jnp.moveaxis(out, 0, 1).reshape(B, S, H, Dh)

def fox_dsa_heads(hn, w_in, b_forget, fox_qn, fox_kn, dsa_qn, dsa_kn, cos, sin):
    B, S, _ = hn.shape
    fq, fk, fv, f_logit, dq, dk, dv, iq, ik, iw = jnp.split(hn @ w_in, EVEN_OFFSETS, axis=-1)
    fq = rms_norm(fq.reshape(B, S, FOX_HEADS, HEAD_DIM), fox_qn)
    fk = rms_norm(fk.reshape(B, S, FOX_HEADS, HEAD_DIM), fox_kn)
    fv = fv.reshape(B, S, FOX_HEADS, HEAD_DIM)
    log_f = jax.nn.log_sigmoid(f_logit.astype(jnp.float32) + b_forget.astype(jnp.float32))
    fox_out = forgetting_attention(fq, fk, fv, log_f)
    dq = partial_rope(rms_norm(dq.reshape(B, S, DSA_HEADS, HEAD_DIM), dsa_qn), cos, sin)
    dk = partial_rope(rms_norm(dk.reshape(B, S, DSA_HEADS, HEAD_DIM), dsa_kn), cos, sin)
    dv = dv.reshape(B, S, DSA_HEADS, HEAD_DIM)
    iq = partial_rope(iq.reshape(B, S, IDX_HEADS, IDX_DIM), cos, sin)
    ik = partial_rope(ik.reshape(B, S, 1, IDX_DIM), cos, sin)[:, :, 0]
    dsa_out = dsa_attention(dq, dk, dv, iq, ik, iw)
    return jnp.concatenate([fox_out.reshape(B, S, FOX_W), dsa_out.reshape(B, S, DSA_W)], axis=-1)

def moba_heads(hn, w_in, moba_qn, moba_kn, cos, sin):
    B, S, _ = hn.shape
    q, k, v = jnp.split(hn @ w_in, 3, axis=-1)
    q = partial_rope(rms_norm(q.reshape(B, S, MOBA_HEADS, HEAD_DIM), moba_qn), cos, sin)
    k = partial_rope(rms_norm(k.reshape(B, S, MOBA_HEADS, HEAD_DIM), moba_kn), cos, sin)
    v = v.reshape(B, S, MOBA_HEADS, HEAD_DIM)
    return moba_attention(q, k, v).reshape(B, S, MOBA_W)

def memory_cross_attention(h, mem, g_x, g_m, wq, wkv, qn, kn, wo):
    B, S, _ = h.shape
    M = mem.shape[1]
    q = rms_norm((rms_norm(h, g_x) @ wq).reshape(B, S, MEM_HEADS, MEM_HEAD_DIM), qn)
    k, v = jnp.split(rms_norm(mem, g_m) @ wkv, 2, axis=-1)
    k = rms_norm(k.reshape(B, M, MEM_HEADS, MEM_HEAD_DIM), kn)
    v = v.reshape(B, M, MEM_HEADS, MEM_HEAD_DIM)
    s = jnp.einsum('bqhd,bkhd->bhqk', q, k, preferred_element_type=jnp.float32) * (MEM_HEAD_DIM ** -0.5)
    p = jax.nn.softmax(s, axis=-1)
    o = jnp.einsum('bhqk,bkhd->bqhd', p.astype(v.dtype), v)
    return o.reshape(B, S, MEM_W) @ wo

def setup_inputs(seed: int = 0) -> dict:
    key = jax.random.key(seed)
    ks = jax.random.split(key, 32)
    n_even = (DEPTH + 1) // 2
    n_odd = DEPTH // 2

    def dense(k, shape, fan_in):
        return jax.random.normal(k, shape, jnp.float32) * (fan_in ** -0.5)

    def gain(k, shape):
        return 1.0 + 0.02 * jax.random.normal(k, shape, jnp.float32)

    return {
        'x': jax.random.normal(ks[0], (BATCH, SEQ, D_MODEL), jnp.float32),
        'mem': jax.random.normal(ks[1], (BATCH, MEM_TOKENS, D_MODEL), jnp.float32),
        'ffn1_norm': gain(ks[2], (DEPTH, D_MODEL)),
        'ffn1_w_in': dense(ks[3], (DEPTH, D_MODEL, 2 * D_FF), D_MODEL),
        'ffn1_w_out': dense(ks[4], (DEPTH, D_FF, D_MODEL), D_FF),
        'mix_norm': gain(ks[5], (DEPTH, D_MODEL)),
        'even_w_in': dense(ks[6], (n_even, D_MODEL, EVEN_IN), D_MODEL),
        'even_b_forget': jax.random.uniform(ks[7], (n_even, FOX_HEADS), jnp.float32, 1.0, 5.0),
        'fox_q_norm': gain(ks[8], (n_even, HEAD_DIM)),
        'fox_k_norm': gain(ks[9], (n_even, HEAD_DIM)),
        'dsa_q_norm': gain(ks[10], (n_even, HEAD_DIM)),
        'dsa_k_norm': gain(ks[11], (n_even, HEAD_DIM)),
        'odd_w_in': dense(ks[12], (n_odd, D_MODEL, 3 * MOBA_W), D_MODEL),
        'moba_q_norm': gain(ks[13], (n_odd, HEAD_DIM)),
        'moba_k_norm': gain(ks[14], (n_odd, HEAD_DIM)),
        'mix_w_out': dense(ks[15], (DEPTH, MIX_WIDTH, D_MODEL), MIX_WIDTH),
        'mem_norm_x': gain(ks[16], (DEPTH, D_MODEL)),
        'mem_norm_m': gain(ks[17], (DEPTH, D_MODEL)),
        'mem_wq': dense(ks[18], (DEPTH, D_MODEL, MEM_W), D_MODEL),
        'mem_wkv': dense(ks[19], (DEPTH, D_MODEL, 2 * MEM_W), D_MODEL),
        'mem_q_norm': gain(ks[20], (DEPTH, MEM_HEAD_DIM)),
        'mem_k_norm': gain(ks[21], (DEPTH, MEM_HEAD_DIM)),
        'mem_wo': dense(ks[22], (DEPTH, MEM_W, D_MODEL), MEM_W),
        'ffn2_norm': gain(ks[23], (DEPTH, D_MODEL)),
        'ffn2_w_in': dense(ks[24], (DEPTH, D_MODEL, 2 * D_FF), D_MODEL),
        'ffn2_w_out': dense(ks[25], (DEPTH, D_FF, D_MODEL), D_FF),
    }

def reference(x, mem, ffn1_norm, ffn1_w_in, ffn1_w_out, mix_norm, even_w_in, even_b_forget,
              fox_q_norm, fox_k_norm, dsa_q_norm, dsa_k_norm, odd_w_in, moba_q_norm, moba_k_norm,
              mix_w_out, mem_norm_x, mem_norm_m, mem_wq, mem_wkv, mem_q_norm, mem_k_norm, mem_wo,
              ffn2_norm, ffn2_w_in, ffn2_w_out):
    cos, sin = rope_tables(x.shape[1])
    h = x
    for layer in range(DEPTH):
        h = h + 0.5 * swiglu_ffn(h, ffn1_norm[layer], ffn1_w_in[layer], ffn1_w_out[layer])
        hn = rms_norm(h, mix_norm[layer])
        if layer % 2 == 0:
            e = layer // 2
            mixed = fox_dsa_heads(hn, even_w_in[e], even_b_forget[e], fox_q_norm[e], fox_k_norm[e],
                                  dsa_q_norm[e], dsa_k_norm[e], cos, sin)
        else:
            o = layer // 2
            mixed = moba_heads(hn, odd_w_in[o], moba_q_norm[o], moba_k_norm[o], cos, sin)
        h = h + mixed @ mix_w_out[layer]
        h = h + memory_cross_attention(h, mem, mem_norm_x[layer], mem_norm_m[layer], mem_wq[layer],
                                       mem_wkv[layer], mem_q_norm[layer], mem_k_norm[layer], mem_wo[layer])
        h = h + 0.5 * swiglu_ffn(h, ffn2_norm[layer], ffn2_w_in[layer], ffn2_w_out[layer])
    return h


_drawn_inputs = setup_inputs


def setup_inputs(seed=0):
    import zlib

    import numpy as np

    out = dict(_drawn_inputs(seed))
    spreads = {}
    factors = {'ffn1_norm': 3.188,
     'fox_q_norm': 8.0,
     'fox_k_norm': 8.0,
     'dsa_q_norm': 8.0,
     'dsa_k_norm': 8.0,
     'moba_q_norm': 8.0,
     'moba_k_norm': 8.0,
     'mem_norm_x': 8.0,
     'mem_norm_m': 8.0,
     'mem_q_norm': 8.0,
     'mem_k_norm': 8.0,
     'ffn2_norm': 5.412}
    for name, (base, spread) in spreads.items():
        noise = np.random.default_rng([zlib.crc32(name.encode()), seed]).standard_normal(out[name].shape)
        drawn = base * np.exp(spread * noise) if base else spread * noise
        out[name] = __import__('jax').numpy.asarray(drawn.astype(out[name].dtype))
    for name, factor in factors.items():
        out[name] = (out[name] * factor).astype(out[name].dtype)
    return out
```

```python
from contextlib import ExitStack

import numpy as np

import concourse.bass as bass
from concourse import mybir

ALU = mybir.AluOpType
ACT = mybir.ActivationFunctionType
F32 = mybir.dt.float32
F32R = mybir.dt.float32r
BF16 = mybir.dt.bfloat16
AX = mybir.AxisListType

P = 128
D = 1024
T = 2
SEQ = T * P
KC = D // P
FF = 2816
FJ = FF // P
HD = 64
ROT = HD // 4
HALF = ROT // 2
DEPTH = 2
UNIT = 1024
RAW = 12
AHEAD = 6
TOPK = min(256, SEQ // 4)
IDX_HEADS = 8
FOX_HEADS = 8
NEG = -1.0e30
TAKEN = -3.0e38
EPS = 1e-6
SMALL = HD + FOX_HEADS + IDX_HEADS

C_ID, C_TRI, C_ONE, C_NEG, C_COS, C_SIN, C_HALF, C_END = 0, 128, 256, 384, 512, 528, 544, 560

ROWS = ["fox_q", "fox_k", "dsa_q", "dsa_k", "moba_q", "moba_k", "mem_q0", "mem_k0", "mem_q1", "mem_k1"]
ROW_END = HD * len(ROWS) + FOX_HEADS


def ffn_units(l, which):
    order = [("a", 0), ("b", 0)]
    for j in range(1, FJ):
        order += [("a", j), ("b", j), ("o", j - 1)]
    order.append(("o", FJ - 1))
    return [(which + part, l, j) for part, j in order]


def blocks_of(l):
    if l == 0:
        w = FOX_HEADS * HD
        fq, fk, fv, _, dq, dk, dv, iq, _ = np.cumsum([0, w, w, w, FOX_HEADS, w, w, w, IDX_HEADS * HD])
        return [("iq", iq), ("small", None), ("dq", dq), ("dk", dk), ("dv", dv), ("fq", fq), ("fk", fk), ("fv", fv)]
    return [("q0", 0), ("q1", 512), ("k0", 1024), ("k1", 1536), ("v0", 2048), ("v1", 2560)]


def unit_list():
    units, start = [], {}

    def add(name, l, more):
        start[name, l] = len(units)
        units.extend(more)

    for l in range(DEPTH):
        add("memkv", l, [("memkv", l, i) for i in range(4)])
    for l in range(DEPTH):
        add("ffn1", l, ffn_units(l, "ffn1"))
        more = []
        for name, _ in blocks_of(l):
            more += [("small", l, 0)] if name == "small" else [("mix:" + name, l, i) for i in range(4)]
        add("proj", l, more)
        add("mixout", l, [("mixout", l, k) for k in range(KC)])
        add("memq", l, [("memq", l, i) for i in range(2)])
        add("memo", l, [("memo", l, i) for i in range(2)])
        add("ffn2", l, ffn_units(l, "ffn2"))
    return units, start


def build(nc, x, mem, stream, gain_cols, gain_rows, consts, picks, out):
    units, start = unit_list()
    N_UNITS = len(units)
    ctx = ExitStack()

    def sb(name, shape, dt=F32):
        return ctx.enter_context(nc.sbuf_tensor(name, shape, dt))

    def sem(name):
        return ctx.enter_context(nc.semaphore(name))

    raw = sb("raw", [P, RAW, UNIT])
    w_hi = sb("w_hi", [P, AHEAD, UNIT], F32R)
    w_lo = sb("w_lo", [P, AHEAD, UNIT], F32R)
    h = sb("h", [P, T, D])
    memh = sb("memh", [P, T, D])
    t_hi = sb("t_hi", [P, KC, SEQ], F32R)
    t_lo = sb("t_lo", [P, KC, SEQ], F32R)
    g_hi = sb("g_hi", [P, 2, SEQ], F32R)
    g_lo = sb("g_lo", [P, 2, SEQ], F32R)
    heads_raw = sb("heads_raw", [P, 2, T, 512])
    squares = sb("squares", [P, T, 512])
    rope_tmp = sb("rope_tmp", [P, 4, T, 8, HALF])
    qk_t = sb("qk_t", [P, 16, SEQ])
    idx_t = sb("idx_t", [P, 5, SEQ])
    v_tok = sb("v_tok", [P, T, 1024])
    mem_kt = sb("mem_kt", [P, DEPTH, 2, SEQ])
    mem_v = sb("mem_v", [P, DEPTH, T, 256])
    probs = sb("probs", [P, 2, 2, 512])
    small = sb("small", [P, T, 2 * IDX_HEADS])
    forget = sb("forget", [P, 6, T, FOX_HEADS])
    cum_t = sb("cum_t", [FOX_HEADS, SEQ])
    neg_cum_t = sb("neg_cum_t", [FOX_HEADS, SEQ])
    score = sb("score", [P, 384])
    top8 = sb("top8", [P, T, 8])
    sel_mask = sb("sel_mask", [P, 384], BF16)
    ctab = sb("ctab", [P, C_END])
    id_bf = sb("id_bf", [P, P], BF16)
    neg_bf = sb("neg_bf", [P, P], BF16)
    gcols = sb("gcols", [P, 10 * KC])
    grows = sb("grows", [P, ROW_END])
    tok_ss = sb("tok_ss", [P, T])
    tok_ms = sb("tok_ms", [P, T])
    tok_rs = sb("tok_rs", [P, T])
    head_ss = sb("head_ss", [P, T, 8])
    head_ms = sb("head_ms", [P, T, 8])
    head_rs = sb("head_rs", [P, T, 8])
    row_max = sb("row_max", [P, 2, 4])
    row_sum = sb("row_sum", [P, 2, 4])
    row_inv = sb("row_inv", [P, 2, 4])

    g_act = probs[:, 0, 0].rearrange("p (a s) -> p a s", a=2)
    g_f32 = probs[:, 1, 0].rearrange("p (a s) -> p a s", a=2)
    probs_t = heads_raw
    nrm = qk_t[:, 0:8, :].rearrange("p (t c) s -> p t (c s)", t=T)
    relu_d = squares[:, :, 0:384]
    mem_qt = idx_t[:, 0:2, :]
    pick = memh[0:FOX_HEADS].rearrange("p t d -> p (t d)").rearrange("p (n s) -> p n s", n=FOX_HEADS)

    acc = [ctx.enter_context(nc.psum_tensor(f"acc{i}", [P, 512], F32)) for i in range(4)]
    up = [ctx.enter_context(nc.psum_tensor(f"up{i}", [P, 512], F32)) for i in range(2)]
    tr = [ctx.enter_context(nc.psum_tensor(f"tr{i}", [P, 512], F32)) for i in range(2)]

    def turned(phase, c):
        banks = acc if "ffn" in phase else tr + up
        return banks[c % 4][:, (c // 4) * SEQ:(c // 4 + 1) * SEQ]

    raw_landed = [sem(f"raw_landed{i}") for i in range(RAW)]
    hi_ready = sem("hi_ready")
    lo_ready = sem("lo_ready")
    unit_used = sem("unit_used")
    x_landed, mem_landed, tables_landed = sem("x_landed"), sem("mem_landed"), sem("tables_landed")
    picks_landed = sem("picks_landed")
    bf_ready = sem("bf_ready")
    ss_act, ms_ready, rs_ready = sem("ss_act"), sem("ms_ready"), sem("rs_ready")
    scaled_act, scaled_dve = sem("scaled_act"), sem("scaled_dve")
    norm_tr = sem("norm_tr")
    thi_ready, tlo_ready = sem("thi_ready"), sem("tlo_ready")
    silu_done, gate_done = sem("silu_done"), sem("gate_done")
    ghi_done, glo_done = sem("ghi_done"), sem("glo_done")
    h_ready = sem("h_ready")
    proj_taken = sem("proj_taken")
    hms_ready, hrs_ready = sem("hms_ready"), sem("hrs_ready")
    heads_ready = sem("heads_ready")
    heads_tr, heads_stored = sem("heads_tr"), sem("heads_stored")
    dots_done, relu_done, score_done = sem("dots_done"), sem("relu_done"), sem("score_done")
    abs_ready, ln_ready, log_ready = sem("abs_ready"), sem("ln_ready"), sem("log_ready")
    cum_done, cum_stored = sem("cum_done"), sem("cum_stored")
    sel_ready = sem("sel_ready")
    s_done, max_done, exp_done, prob_done = sem("s_done"), sem("max_done"), sem("exp_done"), sem("prob_done")
    ptr_done, pt_stored, pv_done = sem("ptr_done"), sem("pt_stored"), sem("pv_done")
    ohi_done, olo_done = sem("ohi_done"), sem("olo_done")
    act_chain, dve_chain = sem("act_chain"), sem("dve_chain")
    out_stored = sem("out_stored")

    ident = ctab[:, C_ID:C_ID + P]
    tri_ones = ctab[:, C_TRI:C_ONE + P]
    causal = ctab[:, C_NEG:C_NEG + P]
    cos_t = ctab[:, C_COS:C_COS + 16].rearrange("p (t d) -> p t d", t=T)
    sin_t = ctab[:, C_SIN:C_SIN + 16].rearrange("p (t d) -> p t d", t=T)
    halves = ctab[:, C_HALF:C_HALF + 16].rearrange("p (t n) -> p t n", t=T)
    row_of = {n: grows[:, HD * i:HD * (i + 1)] for i, n in enumerate(ROWS)}
    b_forget = grows[:, HD * len(ROWS):ROW_END]

    PROJ = []

    def block(phase, l, first, name, n_units, ncols, **kw):
        b = dict(phase=phase, l=l, first=first, name=name, n_units=n_units, ncols=ncols, i=len(PROJ),
                 nh=0, gain=None, rope=False, scale=False, dst=[], v=None)
        b["q"] = sum(bool(c["nh"]) for c in PROJ)
        b.update(kw)
        PROJ.append(b)

    for l in range(DEPTH):
        block("memkv", l, start["memkv", l], "memkv", 4, 512, nh=4, gain=f"mem_k{l}",
              dst=[mem_kt[:, l]], v=(mem_v[:, l], 256, 256))
    for l in range(DEPTH):
        u = start["proj", l]
        for name, _ in blocks_of(l):
            if name == "iq":
                kw = dict(nh=8, rope=True, dst=[idx_t[:, 0:2], idx_t[:, 2:4]])
            elif name == "small":
                kw = dict(nh=2, rope=True, dst=[idx_t[:, 4:5]])
            elif "v" in name:
                at = {"dv": 0, "fv": 512, "v0": 0, "v1": 512}[name]
                kw = dict(v=(v_tok[:, :, at:at + 512], 0, 512))
            else:
                at = {"dq": 0, "dk": 4, "fq": 8, "fk": 12, "q0": 0, "q1": 4, "k0": 8, "k1": 12}[name]
                kind = {"d": "dsa", "f": "fox"}.get(name[0], "moba")
                part = "q" if "q" in name else "k"
                kw = dict(nh=8, gain=f"{kind}_{part}", rope=kind != "fox", scale=part == "q",
                          dst=[qk_t[:, at:at + 2], qk_t[:, at + 2:at + 4]])
            n = 1 if name == "small" else 4
            block("proj", l, u, name, n, SMALL if name == "small" else 512, **kw)
            u += n
        block("memq", l, start["memq", l], "memq", 2, 256, nh=4, gain=f"mem_q{l}", scale=True, dst=[mem_qt])
    blocks_in = {}
    for b in PROJ:
        blocks_in.setdefault((b["phase"], b["l"]), []).append(b)

    NORM = {("memkv", 0): 0, ("memkv", 1): 1}
    for l in range(DEPTH):
        for i, name in enumerate(("ffn1", "proj", "memq", "ffn2")):
            NORM[name, l] = 2 + 4 * l + i
    FFN = {("ffn1", 0): 0, ("ffn2", 0): 1, ("ffn1", 1): 2, ("ffn2", 1): 3}

    PAIRS, pairs_in = [], {}

    def pairs(kind, l, n, q0, k0, v, o0):
        for i in range(n):
            q, k = (mem_qt[:, i], mem_kt[:, l, i]) if kind == "mem" else (qk_t[:, q0 + i], qk_t[:, k0 + i])
            pairs_in.setdefault((kind, l), []).append(len(PAIRS))
            PAIRS.append(dict(kind=kind, q=q, k=k, v=v[:, :, P * i:P * (i + 1)], head=2 * i, o=o0 + i))

    pairs("fox", 0, 4, 8, 12, v_tok[:, :, 512:1024], 0)
    pairs("dsa", 0, 4, 0, 4, v_tok[:, :, 0:512], 4)
    pairs("mem", 0, 2, 0, 0, mem_v[:, 0], 0)
    pairs("moba", 1, 8, 0, 8, v_tok[:], 0)
    pairs("mem", 1, 2, 0, 0, mem_v[:, 1], 0)
    PAIR_OF = {("mixout", 0): 0, ("memo", 0): 8, ("mixout", 1): 10, ("memo", 1): 18}

    def qtiles(n):
        return [(0, 0, 256), (1, 256, 256)] if PAIRS[n]["kind"] == "mem" else [(0, 0, 128), (1, 128, 256)]

    def cols(n):
        return 512 if PAIRS[n]["kind"] == "mem" else 384

    def steps_of(group):
        ns = pairs_in[group]
        for s in range(len(ns) + 2):
            yield (ns[s] if s < len(ns) else None, ns[s - 1] if 0 <= s - 1 < len(ns) else None,
                   ns[s - 2] if s >= 2 else None)

    LOOPS, PER = (FJ - 2) // 4, 4
    assert LOOPS * PER == FJ - 2 and 3 * PER == RAW

    def up_units(u0, j):
        return u0 + 2 if j == 0 else u0 + 3 * j + 1

    blk = ctx.enter_context(nc.Block())

    @blk.sync
    def _(sp):
        def load(u, slot):
            sp.dma_start(raw[:, slot, :], stream[bass.ds(u, 1)].rearrange("a p f -> p (a f)")).then_inc(raw_landed[slot], 16)

        sp.dma_start(memh[:], mem.rearrange("o (t p) d -> p (o t) d", p=P)).then_inc(mem_landed, 16)
        sp.dma_start(ctab[:], consts).then_inc(tables_landed, 16)
        sp.dma_start(gcols[:], gain_cols).then_inc(tables_landed, 16)
        sp.dma_start(grows[:], gain_rows.broadcast_to([P, ROW_END])).then_inc(tables_landed, 16)
        for u in range(AHEAD):
            load(u, u)
        sp.dma_start(h[:], x.rearrange("o (t p) d -> p (o t) d", p=P)).then_inc(x_landed, 16)
        for u in range(AHEAD, RAW):
            load(u, u)
        sp.wait_ge(norm_tr, 8)
        sp.dma_start(pick, picks.rearrange("p (n s) -> p n s", n=FOX_HEADS)).then_inc(picks_landed, 16)
        with sp.Fori(1, N_UNITS // RAW) as g:
            for slot in range(RAW):
                sp.wait_ge(lo_ready, (g - 1) * RAW + slot + 1)
                load(g * RAW + slot, slot)
        for u in range(N_UNITS // RAW * RAW, N_UNITS):
            sp.wait_ge(lo_ready, u - RAW + 1)
            load(u, u % RAW)
        for t in range(T):
            sp.wait_ge(h_ready, 4 * (4 * DEPTH - 1) + 2 * t + 2)
            sp.dma_start(out.rearrange("o (t p) d -> p (o t) d", p=P)[:, t], h[:, t]).then_inc(out_stored, 16)
        sp.wait_ge(out_stored, 16 * T)

    @blk.gpsimd
    def _(pool):
        pool.wait_ge(tables_landed, 48)

        def norm(phase, l):
            n = NORM[phase, l]
            pool.wait_ge(ms_ready, n + 1)
            nc.gpsimd.tensor_tensor(tok_rs[:], tok_ms[:], halves[:, 0, 0:T], ALU.pow).then_inc(rs_ready, 1)

        def heads(phase, l):
            for b in blocks_in[phase, l]:
                if b["gain"]:
                    k = sum(bool(c["gain"]) for c in PROJ[:b["i"]])
                    pool.wait_ge(hms_ready, k + 1)
                    n = b["nh"]
                    nc.gpsimd.tensor_tensor(head_rs[:, :, 0:n], head_ms[:, :, 0:n], halves[:, :, 0:n],
                                            ALU.pow).then_inc(hrs_ready, 1)

        for l in range(DEPTH):
            norm("memkv", l)
            heads("memkv", l)
        for l in range(DEPTH):
            norm("ffn1", l)
            norm("proj", l)
            heads("proj", l)
            norm("memq", l)
            heads("memq", l)
            norm("ffn2", l)

    @blk.scalar
    def _(act):
        def hi(u, it=0):
            act.wait_ge(raw_landed[u % RAW], it * 16 + 16 * (u // RAW + 1))
            if u >= AHEAD:
                act.wait_ge(unit_used, it * RAW + (u - AHEAD + 1))
            nc.scalar.activation(w_hi[:, u % AHEAD, :], raw[:, u % RAW, :], ACT.Copy).then_inc(hi_ready, 1)

        def ahead(u):
            if u + AHEAD < N_UNITS:
                hi(u + AHEAD)

        def norm(phase, l):
            n = NORM[phase, l]
            src = memh if phase == "memkv" else h
            if phase == "memkv":
                act.wait_ge(mem_landed, 16)
            elif n == 2:
                act.wait_ge(x_landed, 16)
            else:
                act.wait_ge(h_ready, 4 * (n - 3) + 2)
            if n >= 1:
                act.wait_ge(norm_tr, 4 * n)
            nc.scalar.activation(nrm[:, 0, :], src[:, 0, :], ACT.Square, accum_out=tok_ss[:, 0:1]).then_inc(ss_act, 1)
            act.wait_ge(rs_ready, n + 1)
            nc.scalar.activation(nrm[:, 0, :], src[:, 0, :], ACT.Copy, scale=tok_rs[:, 0:1]).then_inc(scaled_act, 1)
            if n == 0:
                act.wait_ge(tables_landed, 48)
            if start[phase, l]:
                act.wait_ge(unit_used, start[phase, l])
            for c in range(KC):
                act.wait_ge(norm_tr, 4 * n + c % 4 + 1)
                if c >= 4:
                    act.wait_ge(tlo_ready, KC * n + c - 3)
                nc.scalar.activation(t_hi[:, c, :], turned(phase, c), ACT.Copy,
                                     scale=gcols[:, n * KC + c:n * KC + c + 1]).then_inc(thi_ready, 1)

        def ffn(phase, l):
            f, u0 = FFN[phase, l], start[phase, l]

            def silu(j, it=0):
                act.wait_ge(unit_used, it * RAW + up_units(u0, j))
                nc.scalar.activation(g_act[:, j % 2, :], up[j % 2][:, 0:SEQ], ACT.Silu).then_inc(silu_done, 1)

            def ghi(j, it=0):
                act.wait_ge(gate_done, it * PER + (FJ * f + j + 1))
                nc.scalar.activation(g_hi[:, j % 2, :], g_f32[:, j % 2, :], ACT.Copy).then_inc(ghi_done, 1)

            ahead(u0)
            ahead(u0 + 1)
            silu(0)
            with act.Fori(0, LOOPS - 1) as it:
                for i in range(PER):
                    u = u0 + 2 + 3 * i
                    ghi(i, it)
                    hi(u + AHEAD, it)
                    hi(u + 1 + AHEAD, it)
                    silu(i + 1, it)
                    hi(u + 2 + AHEAD, it)
            for j in range(FJ - 2 - PER, FJ - 2):
                u = u0 + 2 + 3 * j
                ghi(j)
                ahead(u)
                ahead(u + 1)
                silu(j + 1)
                ahead(u + 2)
            j = FJ - 2
            u = u0 + 2 + 3 * j
            ghi(j)
            ahead(u)
            ahead(u + 1)
            silu(j + 1)
            ghi(j + 1)
            ahead(u + 2)
            ahead(u + 3)

        def take(b):
            act.wait_ge(unit_used, b["first"] + b["n_units"])
            q, w = b["q"], b["nh"] * HD
            if w:
                if q:
                    act.wait_ge(heads_ready, q)
                if q >= 2:
                    act.wait_ge(heads_tr, q - 1)
            for t in range(T):
                ps = acc[2 * (b["i"] % 2) + t]
                if b["gain"]:
                    nc.scalar.activation(squares[:, t, 0:w], ps[:, 0:w], ACT.Square)
                if b["name"] == "small":
                    nc.scalar.activation(heads_raw[:, q % 2, t, 0:HD], ps[:, 0:HD], ACT.Copy)
                    nc.scalar.activation(heads_raw[:, q % 2, t, HD:2 * HD], ps[:, 0:HD], ACT.Copy)
                    last = nc.scalar.activation(small[:, t, :], ps[:, HD:SMALL], ACT.Copy)
                elif w:
                    last = nc.scalar.activation(heads_raw[:, q % 2, t, 0:w], ps[:, 0:w], ACT.Copy)
                if b["v"]:
                    dst, c0, n = b["v"]
                    last = nc.scalar.activation(dst[:, t, :], ps[:, c0:c0 + n], ACT.Copy)
            last.then_inc(proj_taken, 1)

        def store(b):
            act.wait_ge(heads_tr, b["q"] + 1)
            for i, dst in enumerate(b["dst"]):
                n = dst.shape[1]
                last = nc.scalar.activation(dst, tr[i][:, 0:n * SEQ].rearrange("p (a s) -> p a s", a=n), ACT.Copy)
            last.then_inc(heads_stored, 1)

        def project(phase, l):
            prev = None
            for b in blocks_in[phase, l]:
                for i in range(b["n_units"]):
                    ahead(b["first"] + i)
                take(b)
                if prev is not None:
                    store(prev)
                prev = b if b["nh"] else None
                if b["name"] == "small":
                    act.wait_ge(abs_ready, 1)
                    nc.scalar.activation(forget[:, 2], forget[:, 1], ACT.Exp, scale=-1.0).then_inc(act_chain, 1)
                    act.wait_ge(act_chain, 1)
                    nc.scalar.activation(forget[:, 3], forget[:, 2], ACT.Ln, bias=1.0).then_inc(ln_ready, 1)
            if prev is not None:
                store(prev)

        def index_scores():
            for i in range(IDX_HEADS):
                act.wait_ge(dots_done, i + 1)
                if i >= 2:
                    act.wait_ge(score_done, i - 1)
                nc.scalar.activation(relu_d[:, i % 2, :], acc[i % 4][:, 0:384], ACT.Relu,
                                     scale=HD ** -0.5).then_inc(relu_done, 1)

        def attention(group):
            for a, b, c in steps_of(group):
                if a is not None:
                    act.wait_ge(max_done, a + 1)
                    if a >= 2:
                        act.wait_ge(ptr_done, a - 1)
                    for e in range(2):
                        for t, c0, w in qtiles(a):
                            i = 2 * e + t
                            last = nc.scalar.activation(
                                probs[:, a % 2, e, c0:c0 + w], acc[2 * (a % 2) + e][:, c0:c0 + w], ACT.Exp,
                                bias=row_max[:, a % 2, i:i + 1], accum_out=row_sum[:, a % 2, i:i + 1])
                    last.then_inc(exp_done, 1)
                if b is not None:
                    act.wait_ge(ptr_done, b + 1)
                    if b >= 2:
                        act.wait_ge(pv_done, b - 1)
                    for e in range(2):
                        last = nc.scalar.activation(probs_t[:, b % 2, e, 0:cols(b)], up[e][:, 0:cols(b)], ACT.Copy)
                    last.then_inc(pt_stored, 1)
                if c is not None:
                    act.wait_ge(pv_done, c + 1)
                    nc.scalar.activation(t_hi[:, PAIRS[c]["o"], :], tr[c % 2][:, 0:SEQ], ACT.Copy).then_inc(ohi_done, 1)

        for u in range(AHEAD):
            hi(u)
        for l in range(DEPTH):
            norm("memkv", l)
            project("memkv", l)
        for l in range(DEPTH):
            norm("ffn1", l)
            ffn("ffn1", l)
            norm("proj", l)
            project("proj", l)
            if l == 0:
                index_scores()
                attention(("fox", 0))
                attention(("dsa", 0))
            else:
                attention(("moba", 1))
            for i in range(KC):
                ahead(start["mixout", l] + i)
            norm("memq", l)
            project("memq", l)
            attention(("mem", l))
            for i in range(2):
                ahead(start["memo", l] + i)
            norm("ffn2", l)
            ffn("ffn2", l)

    @blk.vector
    def _(dve):
        done = [0]

        def then(ins):
            done[0] += 1
            ins.then_inc(dve_chain, 1)
            dve.wait_ge(dve_chain, done[0])

        def lo(u, it=0):
            dve.wait_ge(hi_ready, it * RAW + (u + 1))
            nc.vector.tensor_tensor(w_lo[:, u % AHEAD, :], raw[:, u % RAW, :], w_hi[:, u % AHEAD, :].bitcast(F32),
                                    ALU.subtract).then_inc(lo_ready, 1)

        def ahead(u):
            if u + AHEAD < N_UNITS:
                lo(u + AHEAD)

        def norm(phase, l):
            n = NORM[phase, l]
            src = memh if phase == "memkv" else h
            if phase == "memkv":
                dve.wait_ge(mem_landed, 16)
            elif n == 2:
                dve.wait_ge(x_landed, 16)
            else:
                dve.wait_ge(h_ready, 4 * (n - 3) + 4)
            if n >= 1:
                dve.wait_ge(norm_tr, 4 * n)
            then(nc.vector.scalar_tensor_tensor(nrm[:, 1, :], src[:, 1, :], 1.0, src[:, 1, :], ALU.mult, ALU.mult,
                                                accum_out=tok_ss[:, 1:2]))
            dve.wait_ge(ss_act, n + 1)
            nc.vector.tensor_scalar(tok_ms[:], tok_ss[:], 1.0 / D, EPS, ALU.mult, ALU.add).then_inc(ms_ready, 1)
            dve.wait_ge(rs_ready, n + 1)
            nc.vector.tensor_scalar(nrm[:, 1, :], src[:, 1, :], tok_rs[:, 1:2], None, ALU.mult).then_inc(scaled_dve, 1)
            for c in range(KC):
                dve.wait_ge(thi_ready, KC * n + c + 1)
                nc.vector.scalar_tensor_tensor(
                    t_lo[:, c, :], turned(phase, c), gcols[:, n * KC + c:n * KC + c + 1], t_hi[:, c, :].bitcast(F32),
                    ALU.mult, ALU.subtract).then_inc(tlo_ready, 1)

        def residual(upto, scale):
            dve.wait_ge(unit_used, upto)
            for t in range(T):
                for c in range(2):
                    half = h[:, t, 512 * c:512 * (c + 1)]
                    nc.vector.scalar_tensor_tensor(half, acc[2 * t + c][:, :], scale, half, ALU.mult,
                                                   ALU.add).then_inc(h_ready, 1)

        def ffn(phase, l):
            f, u0 = FFN[phase, l], start[phase, l]

            def gate(j, it=0):
                dve.wait_ge(silu_done, it * PER + (FJ * f + j + 1))
                nc.vector.tensor_tensor(g_f32[:, j % 2, :], up[j % 2][:, SEQ:2 * SEQ], g_act[:, j % 2, :],
                                        ALU.mult).then_inc(gate_done, 1)

            def glo(j, it=0):
                dve.wait_ge(ghi_done, it * PER + (FJ * f + j + 1))
                nc.vector.tensor_tensor(g_lo[:, j % 2, :], g_f32[:, j % 2, :], g_hi[:, j % 2, :].bitcast(F32),
                                        ALU.subtract).then_inc(glo_done, 1)

            ahead(u0)
            ahead(u0 + 1)
            gate(0)
            with dve.Fori(0, LOOPS - 1) as it:
                for i in range(PER):
                    u = u0 + 2 + 3 * i
                    glo(i, it)
                    lo(u + AHEAD, it)
                    lo(u + 1 + AHEAD, it)
                    gate(i + 1, it)
                    lo(u + 2 + AHEAD, it)
            for j in range(FJ - 2 - PER, FJ - 2):
                u = u0 + 2 + 3 * j
                glo(j)
                ahead(u)
                ahead(u + 1)
                gate(j + 1)
                ahead(u + 2)
            j = FJ - 2
            u = u0 + 2 + 3 * j
            glo(j)
            ahead(u)
            ahead(u + 1)
            gate(j + 1)
            glo(j + 1)
            ahead(u + 2)
            ahead(u + 3)
            residual(u + 4, 0.5)

        def heads(b):
            dve.wait_ge(proj_taken, b["i"] + 1)
            n = b["nh"]
            hr = heads_raw[:, b["q"] % 2, :, 0:n * HD].rearrange("p t (n d) -> p t n d", n=n)
            full = [P, T, n, HD]
            if b["gain"]:
                k = sum(bool(c["gain"]) for c in PROJ[:b["i"]])
                sq = squares[:, :, 0:n * HD].rearrange("p t (n d) -> p t n d", n=n)
                then(nc.vector.tensor_reduce(head_ss[:, :, 0:n], sq, AX.X, ALU.add))
                nc.vector.tensor_scalar(head_ms[:, :, 0:n], head_ss[:, :, 0:n], 1.0 / HD, EPS, ALU.mult,
                                        ALU.add).then_inc(hms_ready, 1)
                dve.wait_ge(hrs_ready, k + 1)
                rs = head_rs[:, :, 0:n]
                if b["scale"]:
                    then(nc.vector.tensor_scalar(rs, rs, HD ** -0.5, None, ALU.mult))
                then(nc.vector.tensor_tensor(hr, hr, rs.unsqueeze(3).broadcast_to(full), ALU.mult))
                gain = nc.vector.tensor_tensor(hr, hr, row_of[b["gain"]].unsqueeze(1).unsqueeze(1).broadcast_to(full),
                                               ALU.mult)
                if not b["rope"]:
                    gain.then_inc(heads_ready, 1)
                    return
                then(gain)
            x1, x2 = hr[:, :, :, 0:HALF], hr[:, :, :, HALF:ROT]
            part = [P, T, n, HALF]
            c, s = (w.unsqueeze(2).broadcast_to(part) for w in (cos_t, sin_t))
            t1, t2, t3, t4 = (rope_tmp[:, i, :, 0:n, :] for i in range(4))
            nc.vector.tensor_tensor(t1, x1, c, ALU.mult)
            nc.vector.tensor_tensor(t2, x2, s, ALU.mult)
            nc.vector.tensor_tensor(t3, x2, c, ALU.mult)
            then(nc.vector.tensor_tensor(t4, x1, s, ALU.mult))
            nc.vector.tensor_tensor(x1, t1, t2, ALU.subtract)
            nc.vector.tensor_tensor(x2, t3, t4, ALU.add).then_inc(heads_ready, 1)

        def forget_gates():
            logits, weights = small[:, :, 0:FOX_HEADS], small[:, :, FOX_HEADS:]
            bias = b_forget.unsqueeze(1).broadcast_to([P, T, FOX_HEADS])
            then(nc.vector.tensor_tensor(forget[:, 0], logits, bias, ALU.add))
            then(nc.vector.tensor_scalar(forget[:, 4], forget[:, 0], -1.0, None, ALU.mult))
            nc.vector.tensor_tensor(forget[:, 1], forget[:, 0], forget[:, 4], ALU.max).then_inc(abs_ready, 1)
            then(nc.vector.tensor_scalar(weights, weights, IDX_HEADS ** -0.5, None, ALU.mult))
            dve.wait_ge(ln_ready, 1)
            nc.vector.scalar_tensor_tensor(forget[:, 5], forget[:, 0], 0.0, forget[:, 3], ALU.min,
                                           ALU.subtract).then_inc(log_ready, 1)

        def project(phase, l):
            for b in blocks_in[phase, l]:
                for i in range(b["n_units"]):
                    ahead(b["first"] + i)
                if b["nh"]:
                    heads(b)
                if b["name"] == "small":
                    forget_gates()
            if (phase, l) == ("proj", 0):
                dve.wait_ge(cum_done, 1)
                nc.vector.tensor_copy(cum_t[:], up[0][0:FOX_HEADS, 0:SEQ])
                nc.vector.tensor_scalar(neg_cum_t[:], up[0][0:FOX_HEADS, 0:SEQ], -1.0, None, ALU.mult).then_inc(cum_stored, 1)

        def index_scores():
            for i in range(IDX_HEADS):
                dve.wait_ge(relu_done, i + 1)
                if i:
                    dve.wait_ge(score_done, i)
                for t, c0, w in ((0, 0, 128), (1, 128, 256)):
                    r, s = relu_d[:, i % 2, c0:c0 + w], score[:, c0:c0 + w]
                    weight = small[:, t, FOX_HEADS + i:FOX_HEADS + i + 1]
                    if i == 0:
                        last = nc.vector.tensor_scalar(s, r, weight, None, ALU.mult)
                    else:
                        last = nc.vector.scalar_tensor_tensor(s, r, weight, s, ALU.mult, ALU.add)
                last.then_inc(score_done, 1)
            dve.wait_ge(score_done, IDX_HEADS)
            nc.vector.tensor_tensor(score[:, 0:128], score[:, 0:128], causal, ALU.add)
            then(nc.vector.tensor_tensor(score[:, 256:384], score[:, 256:384], causal, ALU.add))

        def select(r):
            tiles = (score[:, 0:128], score[:, 128:384])
            nc.vector.max(top8[:, 0, :], tiles[0])
            then(nc.vector.max(top8[:, 1, :], tiles[1]))
            for t in range(T):
                last = nc.vector.match_replace(tiles[t], top8[:, t, :], tiles[t], TAKEN)
            then(last)
            if r == TOPK // 8 - 1:
                nc.vector.tensor_scalar(sel_mask[:], score[:], TAKEN, NEG, ALU.not_equal, ALU.mult).then_inc(sel_ready, 1)

        def attention(group):
            for i, (a, b, c) in enumerate(steps_of(group)):
                if a is not None:
                    dve.wait_ge(s_done, a + 1)
                    if a >= 2:
                        dve.wait_ge(exp_done, a - 1)
                    for e in range(2):
                        s = acc[2 * (a % 2) + e]
                        if PAIRS[a]["kind"] == "mem":
                            last = nc.vector.tensor_reduce(row_max[:, a % 2, 2 * e:2 * e + 2],
                                                           s[:].rearrange("p (t k) -> p t k", t=T), AX.X, ALU.max, negate=True)
                        else:
                            for t, c0, w in qtiles(a):
                                last = nc.vector.tensor_reduce(row_max[:, a % 2, 2 * e + t:2 * e + t + 1],
                                                               s[:, c0:c0 + w], AX.X, ALU.max, negate=True)
                    last.then_inc(max_done, 1)
                if group[0] == "fox":
                    for r in (2 * i, 2 * i + 1):
                        if r < TOPK // 8:
                            select(r)
                if b is not None:
                    dve.wait_ge(exp_done, b + 1)
                    then(nc.vector.reciprocal(row_inv[:, b % 2, :], row_sum[:, b % 2, :]))
                    for e in range(2):
                        for t, c0, w in qtiles(b):
                            p = probs[:, b % 2, e, c0:c0 + w]
                            last = nc.vector.tensor_scalar(p, p, row_inv[:, b % 2, 2 * e + t:2 * e + t + 1], None, ALU.mult)
                    last.then_inc(prob_done, 1)
                if c is not None:
                    dve.wait_ge(ohi_done, c + 1)
                    o = PAIRS[c]["o"]
                    nc.vector.tensor_tensor(t_lo[:, o, :], tr[c % 2][:, 0:SEQ], t_hi[:, o, :].bitcast(F32),
                                            ALU.subtract).then_inc(olo_done, 1)

        for u in range(AHEAD):
            lo(u)
        dve.wait_ge(tables_landed, 48)
        nc.vector.tensor_copy(id_bf[:], ident)
        nc.vector.tensor_copy(neg_bf[:], causal).then_inc(bf_ready, 1)
        for l in range(DEPTH):
            norm("memkv", l)
            project("memkv", l)
        for l in range(DEPTH):
            norm("ffn1", l)
            ffn("ffn1", l)
            norm("proj", l)
            project("proj", l)
            if l == 0:
                index_scores()
                attention(("fox", 0))
                attention(("dsa", 0))
            else:
                attention(("moba", 1))
            for i in range(KC):
                ahead(start["mixout", l] + i)
            residual(start["mixout", l] + KC, 1.0)
            norm("memq", l)
            project("memq", l)
            attention(("mem", l))
            for i in range(2):
                ahead(start["memo", l] + i)
            residual(start["memo", l] + 2, 1.0)
            norm("ffn2", l)
            ffn("ffn2", l)

    @blk.tensor
    def _(pe):
        mm = nc.tensor.matmul

        def split(u, it=0):
            pe.wait_ge(lo_ready, it * RAW + (u + 1))
            return w_hi[:, u % AHEAD, :], w_lo[:, u % AHEAD, :]

        def products(dst, s_hi, s_lo, m_hi, m_lo, start, stop):
            mm(dst, s_hi, m_hi, start=start, stop=False)
            mm(dst, s_hi, m_lo, start=False, stop=False)
            return mm(dst, s_lo, m_hi, start=False, stop=stop)

        def norm(phase, l):
            n = NORM[phase, l]
            if n == 0:
                pe.wait_ge(tables_landed, 48)
            pe.wait_ge(scaled_dve, n + 1)
            pe.wait_ge(scaled_act, n + 1)
            for c in range(4):
                for c in (c, c + 4):
                    for t in range(T):
                        last = nc.tensor.transpose(turned(phase, c)[:, t * P:(t + 1) * P], nrm[:, t, c * P:(c + 1) * P], ident)
                last.then_inc(norm_tr, 1)

        def down(u, s_hi, s_lo, first, final, it=0):
            hi, lo = split(u, it)
            for t in range(T):
                a, b = s_hi[:, t * P:(t + 1) * P], s_lo[:, t * P:(t + 1) * P]
                for c in range(2):
                    mm(acc[2 * t + c][:, :], a, hi[:, 512 * c:512 * (c + 1)], start=first, stop=False)
                for c in range(2):
                    mm(acc[2 * t + c][:, :], a, lo[:, 512 * c:512 * (c + 1)], start=False, stop=False)
                for c in range(2):
                    last = mm(acc[2 * t + c][:, :], b, hi[:, 512 * c:512 * (c + 1)], start=False, stop=final)
            last.then_inc(unit_used, 1)

        def ffn(phase, l):
            f, u0, n = FFN[phase, l], start[phase, l], NORM[phase, l]

            def chunk(j, u, it=0):
                if j >= 2:
                    pe.wait_ge(gate_done, it * PER + (FJ * f + j - 1))
                for half in range(2):
                    hi, lo = split(u + half, it)
                    dst = up[j % 2][:, half * SEQ:(half + 1) * SEQ]
                    for k in range(KC):
                        if j == 0 and half == 0:
                            pe.wait_ge(tlo_ready, KC * n + k + 1)
                        last = products(dst, hi[:, k * P:(k + 1) * P], lo[:, k * P:(k + 1) * P], t_hi[:, k, :],
                                        t_lo[:, k, :], k == 0, k == KC - 1)
                    last.then_inc(unit_used, 1)

            def out_of(j, u, it=0, first=False, final=False):
                pe.wait_ge(glo_done, it * PER + (FJ * f + j + 1))
                down(u, g_hi[:, j % 2, :], g_lo[:, j % 2, :], first, final, it)

            chunk(0, u0)
            for i in range(PER):
                u = u0 + 2 + 3 * i
                chunk(i + 1, u)
                out_of(i, u + 2, first=i == 0)
            with pe.Fori(1, LOOPS) as it:
                for i in range(PER):
                    u = u0 + 2 + 3 * i
                    pe.wait_ge(gate_done, it * PER + (FJ * f + i))
                    chunk_in_loop(i + 1, u, it, f)
                    out_of(i, u + 2, it)
            j = FJ - 2
            u = u0 + 2 + 3 * j
            chunk(j + 1, u)
            out_of(j, u + 2)
            out_of(j + 1, u + 3, final=True)

        def chunk_in_loop(j, u, it, f):
            for half in range(2):
                hi, lo = split(u + half, it)
                dst = up[j % 2][:, half * SEQ:(half + 1) * SEQ]
                for k in range(KC):
                    last = products(dst, hi[:, k * P:(k + 1) * P], lo[:, k * P:(k + 1) * P], t_hi[:, k, :],
                                    t_lo[:, k, :], k == 0, k == KC - 1)
                last.then_inc(unit_used, 1)

        def turn(b):
            pe.wait_ge(heads_ready, b["q"] + 1)
            if b["q"]:
                pe.wait_ge(heads_stored, b["q"])
            for pair in range(b["nh"] // 2):
                for t in range(T):
                    at = (pair % 2) * SEQ + t * P
                    last = nc.tensor.transpose(tr[pair // 2][:, at:at + P],
                                               heads_raw[:, b["q"] % 2, t, pair * P:(pair + 1) * P], ident)
            last.then_inc(heads_tr, 1)

        def project(phase, l):
            n, prev = NORM[phase, l], None
            for b in blocks_in[phase, l]:
                if b["i"] >= 2:
                    pe.wait_ge(proj_taken, b["i"] - 1)
                per, w = KC // b["n_units"], b["ncols"]
                for i in range(b["n_units"]):
                    hi, lo = split(b["first"] + i)
                    if b is blocks_in[phase, l][0]:
                        pe.wait_ge(tlo_ready, KC * n + per * (i + 1))
                    for t in range(T):
                        dst = acc[2 * (b["i"] % 2) + t][:, 0:w]
                        for kk in range(per):
                            k = per * i + kk
                            last = products(dst, t_hi[:, k, t * P:(t + 1) * P], t_lo[:, k, t * P:(t + 1) * P],
                                            hi[:, kk * w:(kk + 1) * w], lo[:, kk * w:(kk + 1) * w], k == 0, k == KC - 1)
                    last.then_inc(unit_used, 1)
                if prev is not None:
                    turn(prev)
                prev = b if b["nh"] else None
            if prev is not None:
                turn(prev)
            pe.wait_ge(proj_taken, blocks_in[phase, l][-1]["i"] + 1)
            pe.wait_ge(heads_stored, sum(bool(b["nh"]) for b in PROJ[:blocks_in[phase, l][-1]["i"] + 1]))

        def cumulate():
            pe.wait_ge(log_ready, 1)
            dst = up[0][0:FOX_HEADS, :]
            mm(dst[:, 0:SEQ], forget[:, 5, 0], tri_ones, start=True, stop=False)
            mm(dst[:, P:SEQ], forget[:, 5, 1], tri_ones[:, 0:P], start=False, stop=True).then_inc(cum_done, 1)

        def index_scores():
            for i in range(IDX_HEADS):
                if i >= 4:
                    pe.wait_ge(relu_done, i - 3)
                e = slice(HD * (i % 2), HD * (i % 2 + 1))
                for t, c0, w in ((0, 0, 128), (1, 128, 256)):
                    last = mm(acc[i % 4][:, c0:c0 + w], idx_t[e, i // 2, t * P:(t + 1) * P], idx_t[e, 4, 0:w],
                              start=True, stop=True)
                last.then_inc(dots_done, 1)
            pe.wait_ge(relu_done, IDX_HEADS)

        def attention(group):
            if group[0] == "fox":
                pe.wait_ge(picks_landed, 16)
                pe.wait_ge(cum_stored, 1)
                pe.wait_ge(bf_ready, 1)
            if group[0] == "dsa":
                pe.wait_ge(sel_ready, 1)
            for a, b, c in steps_of(group):
                if a is not None:
                    pair, kind = PAIRS[a], PAIRS[a]["kind"]
                    if a >= 2:
                        pe.wait_ge(exp_done, a - 1)
                    for e in range(2):
                        rows = slice(HD * e, HD * (e + 1))
                        for t, c0, w in qtiles(a):
                            s = acc[2 * (a % 2) + e]
                            dst, diag = s[:, c0:c0 + w], s[:, c0 + w - P:c0 + w]
                            last = mm(dst, pair["q"][rows, t * P:(t + 1) * P], pair["k"][rows, 0:w], start=True,
                                      stop=kind == "mem")
                            if kind == "mem":
                                continue
                            if kind == "fox":
                                mine = pair["head"] + e
                                mm(dst, cum_t[:, t * P:(t + 1) * P], pick[:, mine, 0:w], start=False, stop=False)
                                mm(dst, pick[:, mine, 0:P], neg_cum_t[:, 0:w], start=False, stop=False)
                            if kind == "dsa":
                                mm(dst, id_bf[:], sel_mask[:, c0:c0 + w], start=False, stop=False)
                            last = mm(diag, id_bf[:], neg_bf[:], start=False, stop=True)
                    last.then_inc(s_done, 1)
                if b is not None:
                    pe.wait_ge(prob_done, b + 1)
                    if b:
                        pe.wait_ge(pt_stored, b)
                    turns = [(0, 0), (128, 128), (256, 256)]
                    if PAIRS[b]["kind"] == "mem":
                        turns = [(0, 0), (256, 128), (128, 256), (384, 384)]
                    for e in range(2):
                        for src, dst in turns:
                            last = nc.tensor.transpose(up[e][:, dst:dst + P], probs[:, b % 2, e, src:src + P], ident)
                    last.then_inc(ptr_done, 1)
                if c is not None:
                    pe.wait_ge(pt_stored, c + 1)
                    if c >= 2:
                        pe.wait_ge(olo_done, c - 1)
                    v, late = PAIRS[c]["v"], SEQ - (cols(c) - SEQ)
                    for e in range(2):
                        rows = slice(HD * e, HD * (e + 1))
                        mm(tr[c % 2][rows, 0:SEQ], v[:, 0, rows], probs_t[:, c % 2, e, 0:SEQ], start=True, stop=False)
                        last = mm(tr[c % 2][rows, late:SEQ], v[:, 1, rows], probs_t[:, c % 2, e, SEQ:cols(c)],
                                  start=False, stop=True)
                    last.then_inc(pv_done, 1)

        def project_out(phase, l, n):
            for k in range(n):
                pe.wait_ge(olo_done, PAIR_OF[phase, l] + k + 1)
                down(start[phase, l] + k, t_hi[:, k, :], t_lo[:, k, :], k == 0, k == n - 1)

        for l in range(DEPTH):
            norm("memkv", l)
            project("memkv", l)
        for l in range(DEPTH):
            norm("ffn1", l)
            ffn("ffn1", l)
            norm("proj", l)
            project("proj", l)
            if l == 0:
                cumulate()
                index_scores()
                attention(("fox", 0))
                attention(("dsa", 0))
            else:
                attention(("moba", 1))
            project_out("mixout", l, KC)
            norm("memq", l)
            project("memq", l)
            attention(("mem", l))
            project_out("memo", l, 2)
            norm("ffn2", l)
            ffn("ffn2", l)

    ctx.close()


def lay_out(a):
    def rows(w):
        return w.reshape(KC, P, -1).transpose(1, 0, 2)

    def ffn(which, l):
        w_in, w_out = a[which + "_w_in"][l], a[which + "_w_out"][l]
        up = w_in.reshape(KC, P, 2, FJ, P).transpose(2, 3, 1, 0, 4).reshape(2, FJ, P, UNIT)
        down = w_out.reshape(FJ, P, UNIT)
        return {which + "a": up[0], which + "b": up[1], which + "o": down}

    made = {}
    for l in range(DEPTH):
        for which in ("ffn1", "ffn2"):
            for name, w in ffn(which, l).items():
                made[name, l] = w
        made["memkv", l] = rows(a["mem_wkv"][l]).reshape(P, 4, UNIT).transpose(1, 0, 2)
        made["memq", l] = rows(a["mem_wq"][l]).reshape(P, 2, UNIT).transpose(1, 0, 2)
        made["memo", l] = a["mem_wo"][l].reshape(2, P, UNIT)
        made["mixout", l] = a["mix_w_out"][l].reshape(KC, P, UNIT)
        w = a["even_w_in"][0] if l == 0 else a["odd_w_in"][0]
        for name, c0 in blocks_of(l):
            if name == "small":
                f0, i0 = 3 * FOX_HEADS * HD, w.shape[1] - HD - IDX_HEADS
                part = rows(np.concatenate([w[:, i0:i0 + HD], w[:, f0:f0 + FOX_HEADS], w[:, i0 + HD:]], axis=1))
                flat = np.ascontiguousarray(part).reshape(P, KC * SMALL)
                made["small", l] = np.concatenate([flat, np.zeros((P, UNIT - KC * SMALL), w.dtype)], axis=1)[None]
            else:
                made["mix:" + name, l] = rows(w[:, c0:c0 + 512]).reshape(P, 4, UNIT).transpose(1, 0, 2)
    units, _ = unit_list()
    stream = np.stack([made[name, l][i] for name, l, i in units])

    norms = [a["mem_norm_m"][0], a["mem_norm_m"][1]]
    for l in range(DEPTH):
        norms += [a["ffn1_norm"][l], a["mix_norm"][l], a["mem_norm_x"][l], a["ffn2_norm"][l]]
    gain_cols = np.concatenate([g.reshape(KC, P).transpose(1, 0) for g in norms], axis=1)
    gain_rows = np.concatenate([a["fox_q_norm"][0], a["fox_k_norm"][0], a["dsa_q_norm"][0], a["dsa_k_norm"][0],
                                a["moba_q_norm"][0], a["moba_k_norm"][0], a["mem_q_norm"][0], a["mem_k_norm"][0],
                                a["mem_q_norm"][1], a["mem_k_norm"][1], a["even_b_forget"][0]])[None]

    f32 = np.float32
    i = np.arange(P)
    pos = np.arange(SEQ, dtype=f32)
    inv = f32(500000.0) ** (-np.arange(0, ROT, 2, dtype=f32) / f32(ROT))
    ang = (pos[:, None] * inv[None, :]).astype(f32)
    consts = np.zeros((P, C_END), f32)
    consts[:, C_ID:C_ID + P] = np.eye(P)
    consts[:, C_TRI:C_TRI + P] = i[:, None] <= i[None, :]
    consts[:, C_ONE:C_ONE + P] = 1.0
    consts[:, C_NEG:C_NEG + P] = np.where(i[None, :] > i[:, None], NEG, 0.0)
    consts[:, C_COS:C_COS + 16] = np.cos(ang).reshape(T, P, 8).transpose(1, 0, 2).reshape(P, 16)
    consts[:, C_SIN:C_SIN + 16] = np.sin(ang).reshape(T, P, 8).transpose(1, 0, 2).reshape(P, 16)
    consts[:, C_HALF:] = -0.5
    picks = np.zeros((FOX_HEADS, FOX_HEADS, SEQ), f32)
    picks[np.arange(FOX_HEADS), np.arange(FOX_HEADS)] = 1.0
    return {"x": a["x"], "mem": a["mem"], "stream": stream, "gain_cols": gain_cols, "gain_rows": gain_rows,
            "consts": consts, "picks": picks.reshape(FOX_HEADS, -1)}


def kernel(**inputs):
    import numpy as _np
    import concourse.bacc as _bacc
    from concourse import mybir as _mybir
    from concourse.bass_utils import run_bass_kernel_spmd as _run

    a = {k: _np.asarray(v) for k, v in inputs.items()}
    nc = _bacc.Bacc("TRN2", target_bir_lowering=False, num_devices=1)
    arrays, args = {}, []
    for name, v in lay_out(a).items():
        v = _np.ascontiguousarray(v)
        arrays[f"in_{name}_dram"] = v
        args.append(nc.dram_tensor(f"in_{name}_dram", v.shape, _mybir.dt.from_np(v.dtype), kind="ExternalInput").ap())
    args.append(nc.dram_tensor("out_0_dram", (1, SEQ, D), F32, kind="ExternalOutput").ap())
    build(nc, *args)
    r = _run(nc, [arrays], core_ids=[0])
    return r.results[0]["out_0_dram"]
```

```python
from contextlib import ExitStack

import numpy as np

import concourse.bass as bass
from concourse import mybir

ALU = mybir.AluOpType
ACT = mybir.ActivationFunctionType
F32 = mybir.dt.float32
F32R = mybir.dt.float32r
BF16 = mybir.dt.bfloat16
AX = mybir.AxisListType

P = 128
D = 1024
T = 2
SEQ = T * P
KC = D // P
FF = 2816
FJ = FF // P
HD = 64
ROT = HD // 4
HALF = ROT // 2
DEPTH = 2
UNIT = 1024
RAW = 6
AHEAD = 4
ROUND = 12
TOPK = min(256, SEQ // 4)
IDX_HEADS = 8
FOX_HEADS = 8
CUM_LO = HD
CUM_ROWS = CUM_LO + FOX_HEADS
NEG = -1.0e30
TAKEN = -3.0e38
EPS = 1e-6
SMALL = HD + FOX_HEADS + IDX_HEADS

C_ID, C_TRI, C_ONE, C_NEG, C_COS, C_SIN, C_HALF, C_END = 0, 128, 256, 384, 512, 528, 544, 560

HEAD_GAINS = ["fox_q", "fox_k", "dsa_q", "dsa_k", "moba_q", "moba_k", "mem_q0", "mem_k0", "mem_q1", "mem_k1"]
ROTATED = HEAD_GAINS[2:6]
ROW_END = ROT * len(ROTATED) + FOX_HEADS


def ffn_units(l, which):
    order = [("a", 0), ("b", 0)]
    for j in range(1, FJ):
        order += [("a", j), ("b", j), ("o", j - 1)]
    order.append(("o", FJ - 1))
    return [(which + part, l, j) for part, j in order]


def blocks_of(l):
    if l == 0:
        w = FOX_HEADS * HD
        fq, fk, fv, _, dq, dk, dv, iq, _ = np.cumsum([0, w, w, w, FOX_HEADS, w, w, w, IDX_HEADS * HD])
        return [("iq", iq), ("small", None), ("fq", fq), ("fk", fk), ("fv", fv), ("dq", dq), ("dk", dk), ("dv", dv)]
    return [("q0", 0), ("k0", 1024), ("v0", 2048), ("q1", 512), ("k1", 1536), ("v1", 2560)]


def unit_list():
    units, start = [], {}

    def add(name, l, more):
        start[name, l] = len(units)
        units.extend(more)

    for l in range(DEPTH):
        add("ffn1", l, ffn_units(l, "ffn1"))
        more = []
        for name, _ in blocks_of(l):
            more += [("small", l, 0)] if name == "small" else [("mix:" + name, l, i) for i in range(4)]
        add("proj", l, more)
        add("memkv", l, [("memkv", l, i) for i in range(4)])
        add("mixout", l, [("mixout", l, k) for k in range(KC)])
        add("memq", l, [("memq", l, i) for i in range(2)])
        add("memo", l, [("memo", l, i) for i in range(2)])
        add("ffn2", l, ffn_units(l, "ffn2"))
    return units, start


def build(nc, x, mem, stream, gain_cols, gain_rows, consts, picks, out):
    units, start = unit_list()
    N_UNITS = len(units)
    ctx = ExitStack()

    def sb(name, shape, dt=F32):
        return ctx.enter_context(nc.sbuf_tensor(name, shape, dt))

    def sem(name):
        return ctx.enter_context(nc.semaphore(name))

    raw = sb("raw", [P, RAW, UNIT])
    w_hi = sb("w_hi", [P, AHEAD, UNIT], F32R)
    w_lo = sb("w_lo", [P, AHEAD, UNIT], F32R)
    h = sb("h", [P, T, D])
    memh = sb("memh", [P, T, D])
    t_hi = sb("t_hi", [P, KC, SEQ], F32R)
    t_lo = sb("t_lo", [P, KC, SEQ], F32R)
    m_hi = sb("m_hi", [P, KC, SEQ], F32R)
    m_lo = sb("m_lo", [P, KC, SEQ], F32R)
    o_hi = sb("o_hi", [P, KC, SEQ], F32R)
    o_lo = sb("o_lo", [P, KC, SEQ], F32R)
    g_hi = sb("g_hi", [P, 2, SEQ], F32R)
    g_lo = sb("g_lo", [P, 2, SEQ], F32R)
    heads_raw = sb("heads_raw", [P, T, 512])
    squares = sb("squares", [P, T, 512])
    rope_tmp = sb("rope_tmp", [P, 4, T, 8, HALF])
    qk_t = sb("qk_t", [P, 16, SEQ])
    idx_t = sb("idx_t", [P, 5, SEQ])
    v_tok = sb("v_tok", [P, T, 1024])
    mem_kt = sb("mem_kt", [P, 2, SEQ])
    mem_v = sb("mem_v", [P, T, 256])
    probs = sb("probs", [P, 2, 2, 512])
    probs_t = sb("probs_t", [P, 2, 2, 512])
    small = sb("small", [P, T, 2 * IDX_HEADS])
    forget = sb("forget", [P, 6, T, FOX_HEADS])
    cum = sb("cum", [CUM_ROWS, SEQ], F32R)
    neg_cum = sb("neg_cum", [CUM_ROWS, SEQ], F32R)
    pick = sb("pick", [CUM_ROWS, FOX_HEADS, SEQ], F32R)
    relu_d = sb("relu_d", [P, 2, 384])
    score = sb("score", [P, 384])
    top8 = sb("top8", [P, T, 8])
    sel_mask = sb("sel_mask", [P, 384], BF16)
    ctab = sb("ctab", [P, C_END])
    id_bf = sb("id_bf", [P, P], BF16)
    neg_bf = sb("neg_bf", [P, P], BF16)
    gcols = sb("gcols", [P, 10 * KC + len(HEAD_GAINS)])
    rot = sb("rot", [P, len(ROTATED), 4, T, HALF])
    grows = sb("grows", [P, ROW_END])
    tok_ss = sb("tok_ss", [P, T])
    tok_ms = sb("tok_ms", [P, T])
    tok_rs = sb("tok_rs", [P, T])
    mem_ss = sb("mem_ss", [P, T])
    mem_ms = sb("mem_ms", [P, T])
    mem_rs = sb("mem_rs", [P, T])
    head_ss = sb("head_ss", [P, T, 8])
    head_ms = sb("head_ms", [P, T, 8])
    head_rs = sb("head_rs", [P, T, 8])
    row_max = sb("row_max", [P, 2, 4])
    row_sum = sb("row_sum", [P, 2, 4])
    row_inv = sb("row_inv", [P, 2, 4])

    g_act = probs[:, 0, 0].rearrange("p (a s) -> p a s", a=2)
    g_f32 = probs[:, 1, 0].rearrange("p (a s) -> p a s", a=2)
    ab = probs_t[:, :, 0]
    tok_scale = probs_t[:, 0, 1, 0:SEQ]
    diag = probs_t[:, 1, 1, 0:SEQ]
    staged = qk_t[:, 0:8, :].rearrange("p (g a) s -> p g (a s)", g=4).rearrange("p g (c s) -> p g c s", s=P)
    mem_qt = idx_t[:, 0:2, :]
    pick_f32 = v_tok[0:CUM_ROWS].rearrange("p t d -> p (t d)").rearrange("p (n s) -> p n s", n=FOX_HEADS)

    acc = [ctx.enter_context(nc.psum_tensor(f"acc{i}", [P, 512], F32)) for i in range(4)]
    up = [ctx.enter_context(nc.psum_tensor(f"up{i}", [P, 512], F32)) for i in range(2)]
    tr = [ctx.enter_context(nc.psum_tensor(f"tr{i}", [P, 512], F32)) for i in range(2)]

    turned = [bank[:].rearrange("p (c s) -> p c s", s=P) for bank in tr + acc[2:4]]

    def group(ap, g):
        t, c = g // 2, 4 * (g % 2)
        return ap[:, c:c + 4, t * P:(t + 1) * P]

    raw_landed = [sem(f"raw_landed{i}") for i in range(RAW)]
    hi_ready = sem("hi_ready")
    lo_ready = sem("lo_ready")
    unit_used = sem("unit_used")
    x_landed = [sem(f"x_landed{t}") for t in range(T)]
    mem_landed, tables_landed, rows_landed = sem("mem_landed"), sem("tables_landed"), sem("rows_landed")
    picks_landed = sem("picks_landed")
    masks_ready = sem("masks_ready")
    mem_tr, mhi_ready, mlo_ready = sem("mem_tr"), sem("mhi_ready"), sem("mlo_ready")
    ss_act, ms_ready, rs_ready = sem("ss_act"), sem("ms_ready"), sem("rs_ready")
    scaled_act, scaled_dve = sem("scaled_act"), sem("scaled_dve")
    tile_summed = sem("tile_summed")
    norm_tr = sem("norm_tr")
    staged_act, staged_dve = sem("staged_act"), sem("staged_dve")
    thi_ready, tlo_ready = sem("thi_ready"), sem("tlo_ready")
    diag_ready, scale_done, scale_ready = sem("diag_ready"), sem("scale_done"), sem("scale_ready")
    ab_ready = sem("ab_ready")
    silu_done, gate_done = sem("silu_done"), sem("gate_done")
    ghi_done, glo_done = sem("ghi_done"), sem("glo_done")
    h_ready = sem("h_ready")
    tile_done, tile_taken = sem("tile_done"), sem("tile_taken")
    hms_ready, hrs_ready = sem("hms_ready"), sem("hrs_ready")
    heads_ready = sem("heads_ready")
    heads_tr, heads_stored = sem("heads_tr"), sem("heads_stored")
    dots_done, relu_done, score_done = sem("dots_done"), sem("relu_done"), sem("score_done")
    abs_ready, ln_ready, log_ready = sem("abs_ready"), sem("ln_ready"), sem("log_ready")
    cum_done, cum_stored = sem("cum_done"), sem("cum_stored")
    sel_ready = sem("sel_ready")
    s_done, max_done, exp_done, prob_done = sem("s_done"), sem("max_done"), sem("exp_done"), sem("prob_done")
    ptr_done, pt_stored, pv_done = sem("ptr_done"), sem("pt_stored"), sem("pv_done")
    ohi_done, olo_done = sem("ohi_done"), sem("olo_done")
    act_chain, dve_chain = sem("act_chain"), sem("dve_chain")
    out_stored = sem("out_stored")

    ident = ctab[:, C_ID:C_ID + P]
    tri_ones = ctab[:, C_TRI:C_ONE + P]
    causal = ctab[:, C_NEG:C_NEG + P]
    cos_t = ctab[:, C_COS:C_COS + 16].rearrange("p (t d) -> p t d", t=T)
    sin_t = ctab[:, C_SIN:C_SIN + 16].rearrange("p (t d) -> p t d", t=T)
    halves = ctab[:, C_HALF:C_HALF + 16].rearrange("p (t n) -> p t n", t=T)
    head_gain = {n: gcols[:, 10 * KC + i:10 * KC + i + 1] for i, n in enumerate(HEAD_GAINS)}
    b_forget = grows[:, ROT * len(ROTATED):ROW_END]

    PROJ = []

    def block(phase, l, first, name, n_units, ncols, **kw):
        b = dict(phase=phase, l=l, first=first, name=name, n_units=n_units, ncols=ncols, i=len(PROJ),
                 nh=0, gain=None, rope=False, scale=False, dst=[], v=None, bank=2 if name == "small" else 0)
        b["q"] = sum(bool(c["nh"]) for c in PROJ)
        b.update(kw)
        PROJ.append(b)

    for l in range(DEPTH):
        u = start["proj", l]
        for name, _ in blocks_of(l):
            if name == "iq":
                kw = dict(nh=8, rope=True, dst=[idx_t[:, 0:2], idx_t[:, 2:4]])
            elif name == "small":
                kw = dict(nh=2, rope=True, dst=[idx_t[:, 4:5]])
            elif "v" in name:
                at = {"dv": 0, "fv": 512, "v0": 0, "v1": 512}[name]
                kw = dict(v=(v_tok[:, :, at:at + 512], 0, 512))
            else:
                at = {"dq": 0, "dk": 4, "fq": 8, "fk": 12, "q0": 0, "q1": 4, "k0": 8, "k1": 12}[name]
                kind = {"d": "dsa", "f": "fox"}.get(name[0], "moba")
                part = "q" if "q" in name else "k"
                kw = dict(nh=8, gain=f"{kind}_{part}", rope=kind != "fox", scale=part == "q",
                          dst=[qk_t[:, at:at + 2], qk_t[:, at + 2:at + 4]])
            n = 1 if name == "small" else 4
            block("proj", l, u, name, n, SMALL if name == "small" else 512, **kw)
            u += n
        block("memkv", l, start["memkv", l], "memkv", 4, 512, nh=4, gain=f"mem_k{l}", dst=[mem_kt[:]],
              v=(mem_v[:], 256, 256))
        block("memq", l, start["memq", l], "memq", 2, 256, nh=4, gain=f"mem_q{l}", scale=True, dst=[mem_qt])
    BLOCK = {(b["name"], b["l"]): b for b in PROJ}
    for b in PROJ:
        before = [c for c in PROJ[:b["i"]] if c["l"] == b["l"] and c["bank"] == b["bank"]]
        b["before"] = before[-1]["i"] if before and b["name"] != "memq" else None

    NORM = {(name, l): 4 * l + i for l in range(DEPTH) for i, name in enumerate(("ffn1", "proj", "memq", "ffn2"))}
    ROWS_NORM = sorted(NORM, key=NORM.get)
    ROWS_NORM.insert(2, "mem")
    ROWS_NORM = {name: n for n, name in enumerate(ROWS_NORM)}

    def last_of(item):
        return item[0] == "unit" and item[2] == item[1]["n_units"] - 1 and item[1]["name"] != "small"

    FFN = {("ffn1", 0): 0, ("ffn2", 0): 1, ("ffn1", 1): 2, ("ffn2", 1): 3}

    PAIRS, pairs_in = [], {}

    def pairs(kind, l, n, q0, k0, v, o0):
        for i in range(n):
            q, k = (mem_qt[:, i], mem_kt[:, i]) if kind == "mem" else (qk_t[:, q0 + i], qk_t[:, k0 + i])
            pairs_in.setdefault((kind, l), []).append(len(PAIRS))
            PAIRS.append(dict(kind=kind, q=q, k=k, v=v[:, :, P * i:P * (i + 1)], head=2 * i, o=o0 + i,
                              s=acc[0:2] if kind == "mem" and i == 1 else acc[2:4]))

    pairs("fox", 0, 4, 8, 12, v_tok[:, :, 512:1024], 0)
    pairs("dsa", 0, 4, 0, 4, v_tok[:, :, 0:512], 4)
    pairs("mem", 0, 2, 0, 0, mem_v, 0)
    pairs("moba", 1, 8, 0, 8, v_tok[:], 0)
    pairs("mem", 1, 2, 0, 0, mem_v, 0)

    def qtiles(n):
        return [(0, 0, 256), (1, 256, 256)] if PAIRS[n]["kind"] == "mem" else [(0, 0, 128), (1, 128, 256)]

    def cols(n):
        return 512 if PAIRS[n]["kind"] == "mem" else 384

    def attend(ns, s):
        got = [ns[i] if 0 <= i < len(ns) else None for i in (s, s - 1, s - 2)]
        return ("heads", *got)

    def mixing(l):
        items = []

        def units(name, i, *following):
            b = BLOCK[name, l]
            items.append(("unit", b, i))
            items.extend(following)

        if l == 0:
            ns = pairs_in["fox", 0] + pairs_in["dsa", 0]
            step = [attend(ns, s) for s in range(len(ns) + 2)]
            block_named = lambda n: BLOCK[n, 0]
            units("iq", 0, ("mem_rows",))
            units("iq", 1, ("mem_turn", 0, 0, up), ("mem_turn", 1, 0, up))
            units("iq", 2, ("mem_turn", 2, 0, up), ("mem_turn", 3, 0, up))
            units("iq", 3)
            units("small", 0)
            units("fq", 0, ("turn", block_named("iq")), ("take", block_named("small")))
            units("fq", 1)
            units("fq", 2, ("turn", block_named("small")), ("cum",))
            units("fq", 3, ("index", 0))
            units("fk", 0, ("index", 1), ("index", 2))
            units("fk", 1, ("index", 3), ("index", 4))
            units("fk", 2, ("turn", block_named("fq")), ("index", 5))
            units("fk", 3, ("index", 6))
            units("fv", 0, ("index", 7))
            units("fv", 1, ("select", 0))
            units("fv", 2, ("turn", block_named("fk")), step[0])
            units("fv", 3, ("select", 1))
            units("dq", 0, step[1])
            units("dq", 1, ("select", 2))
            units("dq", 2, step[2])
            units("dq", 3, ("select", 3))
            units("dk", 0, ("select", 4))
            units("dk", 1, step[3])
            units("dk", 2, ("turn", block_named("dq")), ("select", 5))
            units("dk", 3, ("select", 6))
            units("dv", 0, ("select", 7))
            units("dv", 1)
            units("dv", 2, ("turn", block_named("dk")), step[4])
            units("dv", 3)
        else:
            ns = pairs_in["moba", 1]
            step = [attend(ns, s) for s in range(len(ns) + 2)]
            block_named = lambda n: BLOCK[n, 1]
            for i in range(4):
                units("q0", i)
            for i in range(4):
                units("k0", i, *([("turn", block_named("q0"))] if i == 2 else []))
            units("v0", 0)
            units("v0", 1)
            units("v0", 2, ("turn", block_named("k0")), step[0])
            units("v0", 3)
            units("q1", 0, step[1])
            units("q1", 1)
            units("q1", 2, step[2])
            units("q1", 3)
            units("k1", 0, step[3])
            units("k1", 1)
            units("k1", 2, ("turn", block_named("q1")))
            units("k1", 3)
            units("v1", 0)
            units("v1", 1)
            units("v1", 2, ("turn", block_named("k1")), step[4])
            units("v1", 3)
        units("memkv", 0, step[5])
        units("memkv", 1, step[6])
        units("memkv", 2, step[7])
        units("memkv", 3)
        for k in range(KC):
            items.append(("out", "mixout", l, k))
            if k in (1, 3):
                items.append(step[8 + k // 2])
            if k == 4:
                items.append(("turn", BLOCK["memkv", l]))
        return spread(items)

    def crossing(l):
        ns = pairs_in["mem", l]
        step = [attend(ns, s) for s in range(4)]
        items = [("unit", BLOCK["memq", l], 0), ("unit", BLOCK["memq", l], 1)]
        if l == 0:
            items += [("mem_turn", i, 1, acc[2:4]) for i in range(4)]
        items += [("mean", BLOCK["memq", l]), ("scale", BLOCK["memq", l]), ("turn", BLOCK["memq", l])]
        return items + [step[0], step[1], step[2], ("out", "memo", l, 0), step[3], ("out", "memo", l, 1)]

    def spread(items):
        got, due = [], []
        for item in items:
            got.append(item)
            if item[0] in ("unit", "out"):
                got.extend(due)
                due = []
            if last_of(item) and item[1]["nh"]:
                b = item[1]
                due = ([("mean", b), ("scale", b)] if b["gain"] else []) + ([("rotate", b)] if b["rope"] else [])
                got.append(due.pop(0))
        assert not due
        return got

    ORDER = {("mix", l): mixing(l) for l in range(DEPTH)} | {("cross", l): crossing(l) for l in range(DEPTH)}
    STAGES = [(name, l) for l in range(DEPTH) for name in ("mix", "cross")]
    BEFORE, pv, turns, quarters = {}, 0, 0, 0
    for stage in STAGES:
        for i, item in enumerate(ORDER[stage]):
            BEFORE[stage, i] = dict(pv=pv, turns=turns, quarters=quarters)
            pv += item[0] == "heads" and item[3] is not None
            turns += item[0] == "turn"
            quarters += item[0] == "mem_turn"

    LOOPS, PER = (FJ - 2) // 4, 4
    assert LOOPS * PER == FJ - 2 and 3 * PER == ROUND and ROUND % RAW == 0 and ROUND % AHEAD == 0

    def up_units(u0, j):
        return u0 + 2 if j == 0 else u0 + 3 * j + 1

    blk = ctx.enter_context(nc.Block())

    @blk.sync
    def _(sp):
        def load(u, slot):
            sp.dma_start(raw[:, slot, :], stream[bass.ds(u, 1)].rearrange("a p f -> p (a f)")).then_inc(raw_landed[slot], 16)

        for t in range(T):
            sp.dma_start(h[:, t], x.rearrange("o (t p) d -> p (o t) d", p=P)[:, t]).then_inc(x_landed[t], 16)
        sp.dma_start(ctab[:], consts).then_inc(tables_landed, 16)
        sp.dma_start(gcols[:], gain_cols).then_inc(tables_landed, 16)
        for u in range(RAW):
            load(u, u)
        sp.dma_start(grows[:], gain_rows.broadcast_to([P, ROW_END])).then_inc(rows_landed, 16)
        sp.dma_start(pick_f32, picks.rearrange("p (n s) -> p n s", n=FOX_HEADS)).then_inc(picks_landed, 16)
        sp.dma_start(memh[:], mem.rearrange("o (t p) d -> p (o t) d", p=P)).then_inc(mem_landed, 16)
        with sp.Fori(1, N_UNITS // RAW) as g:
            for slot in range(RAW):
                sp.wait_ge(lo_ready, (g - 1) * RAW + slot + 1)
                load(g * RAW + slot, slot)
        for u in range(N_UNITS // RAW * RAW, N_UNITS):
            sp.wait_ge(lo_ready, u - RAW + 1)
            load(u, u % RAW)
        for t in range(T):
            sp.wait_ge(h_ready, 4 * (4 * DEPTH - 1) + 2 * t + 2)
            sp.dma_start(out.rearrange("o (t p) d -> p (o t) d", p=P)[:, t], h[:, t]).then_inc(out_stored, 16)
        sp.wait_ge(out_stored, 16 * T)

    @blk.gpsimd
    def _(pool):
        pool.wait_ge(tables_landed, 32)

        def norm(name):
            pool.wait_ge(ms_ready, ROWS_NORM[name] + 1)
            ms, rs = (mem_ms, mem_rs) if name == "mem" else (tok_ms, tok_rs)
            nc.gpsimd.tensor_tensor(rs[:], ms[:], halves[:, 0, 0:T], ALU.pow).then_inc(rs_ready, 1)

        def heads(b):
            pool.wait_ge(hms_ready, sum(bool(c["gain"]) for c in PROJ[:b["i"]]) + 1)
            n = b["nh"]
            nc.gpsimd.tensor_tensor(head_rs[:, :, 0:n], head_ms[:, :, 0:n], halves[:, :, 0:n],
                                    ALU.pow).then_inc(hrs_ready, 1)

        def stage(name, l):
            for item in ORDER[name, l]:
                if item[0] == "mem_rows":
                    norm("mem")
                if item[0] == "mean":
                    heads(item[1])

        for l in range(DEPTH):
            norm(("ffn1", l))
            norm(("proj", l))
            stage("mix", l)
            norm(("memq", l))
            stage("cross", l)
            norm(("ffn2", l))

    @blk.scalar
    def _(act):
        def hi(u, it=0):
            act.wait_ge(raw_landed[u % RAW], it * (16 * ROUND // RAW) + 16 * (u // RAW + 1))
            if u >= AHEAD:
                act.wait_ge(unit_used, it * ROUND + (u - AHEAD + 1))
            nc.scalar.activation(w_hi[:, u % AHEAD, :], raw[:, u % RAW, :], ACT.Copy).then_inc(hi_ready, 1)

        def ahead(u):
            if u + AHEAD < N_UNITS:
                hi(u + AHEAD)

        def mem_rows():
            n = ROWS_NORM["mem"]
            act.wait_ge(mem_landed, 16)
            nc.scalar.activation(probs[:, 0].rearrange("p e s -> p (e s)"), memh[:, 0, :], ACT.Square,
                                 accum_out=mem_ss[:, 0:1]).then_inc(ss_act, 1)
            act.wait_ge(rs_ready, n + 1)
            nc.scalar.activation(memh[:, 0, :], memh[:, 0, :], ACT.Copy, scale=mem_rs[:, 0:1]).then_inc(scaled_act, 1)

        def norm(phase, l):
            n = NORM[phase, l]
            gains = gcols[:, (n + 2) * KC:(n + 3) * KC]

            def stage_group(g):
                act.wait_ge(norm_tr, 4 * n + g + 1)
                for c in range(4):
                    k = 4 * (g % 2) + c
                    last = nc.scalar.activation(staged[:, g, c], turned[g][:, c], ACT.Copy, scale=gains[:, k:k + 1])
                last.then_inc(staged_act, 1)

            def hi_group(g):
                if g % 2 == 0:
                    act.wait_ge(staged_dve, 2 * n + g // 2 + 1)
                else:
                    act.wait_ge(staged_act, 2 * n + g // 2 + 1)
                nc.scalar.activation(group(t_hi, g), staged[:, g], ACT.Copy).then_inc(thi_ready, 1)

            stage_group(1)
            if n:
                act.wait_ge(unit_used, start[phase, l])
            hi_group(0)
            hi_group(1)
            if n == 0:
                act.wait_ge(x_landed[0], 16)
            else:
                act.wait_ge(h_ready, 4 * (n - 1) + 2)
            nc.scalar.activation(squares[:].rearrange("p t d -> p (t d)"), h[:, 0, :], ACT.Square,
                                 accum_out=tok_ss[:, 0:1]).then_inc(ss_act, 1)
            stage_group(3)
            hi_group(2)
            hi_group(3)

        def ffn(phase, l):
            f, u0 = FFN[phase, l], start[phase, l]

            def silu(j, it=0):
                act.wait_ge(ab_ready, it * PER + (FJ * f + j + 1))
                nc.scalar.activation(g_act[:, j % 2, :], ab[:, j % 2, 0:SEQ], ACT.Silu).then_inc(silu_done, 1)

            def ghi(j, it=0):
                act.wait_ge(gate_done, it * PER + (FJ * f + j + 1))
                nc.scalar.activation(g_hi[:, j % 2, :], g_f32[:, j % 2, :], ACT.Copy).then_inc(ghi_done, 1)

            ahead(u0)
            act.wait_ge(scale_done, f + 1)
            nc.scalar.activation(tok_scale, tr[0][:, 0:SEQ], ACT.Copy).then_inc(scale_ready, 1)
            ahead(u0 + 1)
            silu(0)
            with act.Fori(0, LOOPS - 1) as it:
                for i in range(PER):
                    u = u0 + 2 + 3 * i
                    ghi(i, it)
                    hi(u + AHEAD, it)
                    hi(u + 1 + AHEAD, it)
                    silu(i + 1, it)
                    hi(u + 2 + AHEAD, it)
            for j in range(FJ - 2 - PER, FJ - 2):
                u = u0 + 2 + 3 * j
                ghi(j)
                ahead(u)
                ahead(u + 1)
                silu(j + 1)
                ahead(u + 2)
            j = FJ - 2
            u = u0 + 2 + 3 * j
            ghi(j)
            ahead(u)
            ahead(u + 1)
            silu(j + 1)
            ghi(j + 1)
            ahead(u + 2)
            ahead(u + 3)

        def take(b):
            q, w = b["q"], b["nh"] * HD
            for t in range(T):
                if t == 0:
                    act.wait_ge(tile_done, b["i"] + 1)
                else:
                    act.wait_ge(unit_used, b["first"] + b["n_units"])
                if w and q and t == 0:
                    act.wait_ge(heads_tr, q)
                ps = acc[b["bank"] + t]
                rs = 1.0
                if b["name"] != "memkv":
                    rs = tok_rs[:, t:t + 1]
                    act.wait_ge(rs_ready, ROWS_NORM["memq" if b["name"] == "memq" else "proj", b["l"]] + 1)
                if b["gain"]:
                    nc.scalar.activation(squares[:, t, 0:w], ps[:, 0:w], ACT.Square, scale=rs)
                if b["name"] == "small":
                    nc.scalar.activation(heads_raw[:, t, 0:HD], ps[:, 0:HD], ACT.Copy, scale=rs)
                    nc.scalar.activation(heads_raw[:, t, HD:2 * HD], ps[:, 0:HD], ACT.Copy, scale=rs)
                    last = nc.scalar.activation(small[:, t, :], ps[:, HD:SMALL], ACT.Copy, scale=rs)
                elif w:
                    last = nc.scalar.activation(heads_raw[:, t, 0:w], ps[:, 0:w], ACT.Copy, scale=rs)
                if b["v"]:
                    dst, c0, n = b["v"]
                    last = nc.scalar.activation(dst[:, t, :], ps[:, c0:c0 + n], ACT.Copy, scale=rs)
                last.then_inc(tile_taken, 1)
            if b["name"] == "small":
                act.wait_ge(abs_ready, 1)
                nc.scalar.activation(forget[:, 2], forget[:, 1], ACT.Exp, scale=-1.0).then_inc(act_chain, 1)
                act.wait_ge(act_chain, 1)
                nc.scalar.activation(forget[:, 3], forget[:, 2], ACT.Ln, bias=1.0).then_inc(ln_ready, 1)

        def store(b):
            act.wait_ge(heads_tr, b["q"] + 1)
            for i, dst in enumerate(b["dst"]):
                n = dst.shape[1]
                last = nc.scalar.activation(dst, tr[i][:, 0:n * SEQ].rearrange("p (a s) -> p a s", a=n), ACT.Copy,
                                            scale=head_gain[b["gain"]] if b["gain"] else 1.0)
            last.then_inc(heads_stored, 1)

        def mem_turn(i, l, banks, before):
            act.wait_ge(mem_tr, before + 1)
            if l:
                act.wait_ge(unit_used, start["memkv", l - 1] + 4)
            for c in (2 * i, 2 * i + 1):
                last = nc.scalar.activation(m_hi[:, c, :], banks[i % 2][:, (c % 2) * SEQ:(c % 2 + 1) * SEQ], ACT.Copy,
                                            scale=gcols[:, l * KC + c:l * KC + c + 1])
            last.then_inc(mhi_ready, 1)

        def index(i):
            act.wait_ge(dots_done, i + 1)
            if i >= 2:
                act.wait_ge(score_done, i - 1)
            nc.scalar.activation(relu_d[:, i % 2, :], acc[2 + i % 2][:, 0:384], ACT.Relu,
                                 scale=HD ** -0.5).then_inc(relu_done, 1)

        def heads(a, b, c):
            if a is not None:
                act.wait_ge(max_done, a + 1)
                if a >= 2:
                    act.wait_ge(ptr_done, a - 1)
                for e in range(2):
                    for t, c0, w in qtiles(a):
                        i = 2 * e + t
                        last = nc.scalar.activation(
                            probs[:, a % 2, e, c0:c0 + w], PAIRS[a]["s"][e][:, c0:c0 + w], ACT.Exp,
                            bias=row_max[:, a % 2, i:i + 1], accum_out=row_sum[:, a % 2, i:i + 1])
                last.then_inc(exp_done, 1)
            if b is not None:
                act.wait_ge(ptr_done, b + 1)
                if b >= 2:
                    act.wait_ge(pv_done, b - 1)
                for e in range(2):
                    last = nc.scalar.activation(probs_t[:, b % 2, e, 0:cols(b)], up[e][:, 0:cols(b)], ACT.Copy)
                last.then_inc(pt_stored, 1)
            if c is not None:
                act.wait_ge(pv_done, c + 1)
                nc.scalar.activation(o_hi[:, PAIRS[c]["o"], :], tr[c % 2][:, 0:SEQ], ACT.Copy).then_inc(ohi_done, 1)

        def stage(name, l):
            for n, item in enumerate(ORDER[name, l]):
                kind, *args = item
                if kind == "unit":
                    if last_of(item):
                        take(args[0])
                    ahead(args[0]["first"] + args[1])
                elif kind == "take":
                    take(*args)
                elif kind == "turn":
                    store(*args)
                elif kind == "mem_rows":
                    mem_rows()
                elif kind == "mem_turn":
                    mem_turn(*args, BEFORE[(name, l), n]["quarters"])
                elif kind == "index":
                    index(*args)
                elif kind == "heads":
                    heads(*args)
                elif kind == "out":
                    phase, l, k = args
                    ahead(start[phase, l] + k)

        hi(0)
        hi(1)
        norm("ffn1", 0)
        for u in range(2, AHEAD):
            hi(u)
        ffn("ffn1", 0)
        for l in range(DEPTH):
            if l:
                norm("ffn1", l)
                ffn("ffn1", l)
            norm("proj", l)
            stage("mix", l)
            norm("memq", l)
            stage("cross", l)
            norm("ffn2", l)
            ffn("ffn2", l)

    @blk.vector
    def _(dve):
        done = [0]

        def then(ins):
            done[0] += 1
            ins.then_inc(dve_chain, 1)
            dve.wait_ge(dve_chain, done[0])

        def lo(u, it=0):
            dve.wait_ge(hi_ready, it * ROUND + (u + 1))
            nc.vector.tensor_tensor(w_lo[:, u % AHEAD, :], raw[:, u % RAW, :], w_hi[:, u % AHEAD, :].bitcast(F32),
                                    ALU.subtract).then_inc(lo_ready, 1)

        def ahead(u):
            if u + AHEAD < N_UNITS:
                lo(u + AHEAD)

        def square_sums(name, src, junk, ss, ms):
            then(nc.vector.scalar_tensor_tensor(junk, src, 1.0, src, ALU.mult, ALU.mult, accum_out=ss[:, 1:2]))
            dve.wait_ge(ss_act, ROWS_NORM[name] + 1)
            nc.vector.tensor_scalar(ms[:], ss[:], 1.0 / D, EPS, ALU.mult, ALU.add).then_inc(ms_ready, 1)

        def mem_rows():
            dve.wait_ge(mem_landed, 16)
            square_sums("mem", memh[:, 1, :], probs[:, 1].rearrange("p e s -> p (e s)"), mem_ss, mem_ms)
            dve.wait_ge(rs_ready, ROWS_NORM["mem"] + 1)
            nc.vector.tensor_scalar(memh[:, 1, :], memh[:, 1, :], mem_rs[:, 1:2], None, ALU.mult).then_inc(scaled_dve, 1)

        def residual(n, upto, scale):
            for t in range(T):
                if t == 0:
                    dve.wait_ge(tile_summed, n)
                else:
                    dve.wait_ge(unit_used, upto)
                for c in range(2):
                    half = h[:, t, 512 * c:512 * (c + 1)]
                    nc.vector.scalar_tensor_tensor(half, acc[2 * t + c][:, :], scale, half, ALU.mult,
                                                   ALU.add).then_inc(h_ready, 1)

        def norm(phase, l):
            n = NORM[phase, l]
            gains = gcols[:, (n + 2) * KC:(n + 3) * KC]

            def stage_group(g):
                dve.wait_ge(norm_tr, 4 * n + g + 1)
                k = 4 * (g % 2)
                nc.vector.tensor_tensor(staged[:, g], turned[g], gains[:, k:k + 4].unsqueeze(2).broadcast_to([P, 4, P]),
                                        ALU.mult).then_inc(staged_dve, 1)

            def lo_group(g):
                dve.wait_ge(thi_ready, 4 * n + g + 1)
                nc.vector.tensor_tensor(group(t_lo, g), staged[:, g], group(t_hi, g).bitcast(F32),
                                        ALU.subtract).then_inc(tlo_ready, 1)

            stage_group(0)
            lo_group(0)
            stage_group(2)
            lo_group(1)
            if n:
                ahead(start[phase, l] - 1)
            lo_group(2)
            lo_group(3)
            if n == 0:
                dve.wait_ge(x_landed[1], 16)
            else:
                dve.wait_ge(h_ready, 4 * n)
            square_sums((phase, l), h[:, 1, :], heads_raw[:].rearrange("p t d -> p (t d)"), tok_ss, tok_ms)
            if "ffn" in phase:
                dve.wait_ge(rs_ready, ROWS_NORM[phase, l] + 1)
                for t in range(T):
                    last = nc.vector.tensor_scalar(diag[:, t * P:(t + 1) * P], ident, tok_rs[:, t:t + 1], None, ALU.mult)
                last.then_inc(diag_ready, 1)

        def ffn(phase, l):
            f, u0 = FFN[phase, l], start[phase, l]

            def over_rms(j, it=0):
                dve.wait_ge(unit_used, it * ROUND + up_units(u0, j))
                nc.vector.tensor_tensor(ab[:, j % 2].rearrange("p (a s) -> p a s", a=2),
                                        up[j % 2][:].rearrange("p (a s) -> p a s", a=2),
                                        tok_scale.unsqueeze(1).broadcast_to([P, 2, SEQ]), ALU.mult).then_inc(ab_ready, 1)

            def gate(j, it=0):
                dve.wait_ge(silu_done, it * PER + (FJ * f + j + 1))
                nc.vector.tensor_tensor(g_f32[:, j % 2, :], ab[:, j % 2, SEQ:2 * SEQ], g_act[:, j % 2, :],
                                        ALU.mult).then_inc(gate_done, 1)

            def glo(j, it=0):
                dve.wait_ge(ghi_done, it * PER + (FJ * f + j + 1))
                nc.vector.tensor_tensor(g_lo[:, j % 2, :], g_f32[:, j % 2, :], g_hi[:, j % 2, :].bitcast(F32),
                                        ALU.subtract).then_inc(glo_done, 1)

            ahead(u0)
            dve.wait_ge(scale_ready, f + 1)
            over_rms(0)
            ahead(u0 + 1)
            gate(0)
            with dve.Fori(0, LOOPS - 1) as it:
                for i in range(PER):
                    u = u0 + 2 + 3 * i
                    glo(i, it)
                    lo(u + AHEAD, it)
                    over_rms(i + 1, it)
                    lo(u + 1 + AHEAD, it)
                    gate(i + 1, it)
                    lo(u + 2 + AHEAD, it)
            for j in range(FJ - 2 - PER, FJ - 2):
                u = u0 + 2 + 3 * j
                glo(j)
                ahead(u)
                over_rms(j + 1)
                ahead(u + 1)
                gate(j + 1)
                ahead(u + 2)
            j = FJ - 2
            u = u0 + 2 + 3 * j
            glo(j)
            ahead(u)
            over_rms(j + 1)
            ahead(u + 1)
            gate(j + 1)
            glo(j + 1)
            ahead(u + 2)
            residual(NORM[phase, l] + 1, u + 4, 0.5)

        def heads_of(b, taken=False):
            if taken:
                dve.wait_ge(tile_taken, T * (b["i"] + 1))
            return heads_raw[:, :, 0:b["nh"] * HD].rearrange("p t (n d) -> p t n d", n=b["nh"])

        def mean(b):
            dve.wait_ge(tile_taken, T * (b["i"] + 1))
            n = b["nh"]
            sq = squares[:, :, 0:n * HD].rearrange("p t (n d) -> p t n d", n=n)
            then(nc.vector.tensor_reduce(head_ss[:, :, 0:n], sq, AX.X, ALU.add))
            nc.vector.tensor_scalar(head_ms[:, :, 0:n], head_ss[:, :, 0:n], 1.0 / HD, EPS, ALU.mult,
                                    ALU.add).then_inc(hms_ready, 1)

        def scale(b):
            n, hr = b["nh"], heads_of(b)
            dve.wait_ge(hrs_ready, sum(bool(c["gain"]) for c in PROJ[:b["i"]]) + 1)
            rs = head_rs[:, :, 0:n]
            if b["scale"]:
                then(nc.vector.tensor_scalar(rs, rs, HD ** -0.5, None, ALU.mult))
            last = nc.vector.tensor_tensor(hr, hr, rs.unsqueeze(3).broadcast_to([P, T, n, HD]), ALU.mult)
            if b["rope"]:
                then(last)
            else:
                last.then_inc(heads_ready, 1)

        def rotation_tables():
            for i, name in enumerate(ROTATED):
                for half in range(2):
                    row = grows[:, ROT * i + HALF * half:ROT * i + HALF * (half + 1)]
                    row = row.unsqueeze(1).broadcast_to([P, T, HALF])
                    for k, table in enumerate((cos_t, sin_t)):
                        last = nc.vector.tensor_tensor(rot[:, i, 2 * half + k], table, row, ALU.mult)
            then(last)

        def rotate(b):
            n, hr = b["nh"], heads_of(b, not b["gain"])
            x1, x2 = hr[:, :, :, 0:HALF], hr[:, :, :, HALF:ROT]
            part = [P, T, n, HALF]
            if b["gain"]:
                tables = (rot[:, ROTATED.index(b["gain"]), k] for k in range(4))
            else:
                tables = (cos_t, sin_t, cos_t, sin_t)
            c1, s1, c2, s2 = (w.unsqueeze(2).broadcast_to(part) for w in tables)
            t1, t2, t3, t4 = (rope_tmp[:, i, :, 0:n, :] for i in range(4))
            nc.vector.tensor_tensor(t1, x1, c1, ALU.mult)
            nc.vector.tensor_tensor(t2, x2, s2, ALU.mult)
            nc.vector.tensor_tensor(t3, x2, c2, ALU.mult)
            then(nc.vector.tensor_tensor(t4, x1, s1, ALU.mult))
            nc.vector.tensor_tensor(x1, t1, t2, ALU.subtract)
            nc.vector.tensor_tensor(x2, t3, t4, ALU.add).then_inc(heads_ready, 1)

        def forget_gates():
            logits, weights = small[:, :, 0:FOX_HEADS], small[:, :, FOX_HEADS:]
            bias = b_forget.unsqueeze(1).broadcast_to([P, T, FOX_HEADS])
            then(nc.vector.tensor_tensor(forget[:, 0], logits, bias, ALU.add))
            then(nc.vector.tensor_scalar(forget[:, 4], forget[:, 0], -1.0, None, ALU.mult))
            nc.vector.tensor_tensor(forget[:, 1], forget[:, 0], forget[:, 4], ALU.max).then_inc(abs_ready, 1)
            then(nc.vector.tensor_scalar(weights, weights, IDX_HEADS ** -0.5, None, ALU.mult))
            dve.wait_ge(ln_ready, 1)
            nc.vector.scalar_tensor_tensor(forget[:, 5], forget[:, 0], 0.0, forget[:, 3], ALU.min,
                                           ALU.subtract).then_inc(log_ready, 1)

        def cumulated():
            dve.wait_ge(cum_done, 1)
            sums, lo_rows = up[0][0:FOX_HEADS, 0:SEQ], slice(CUM_LO, CUM_ROWS)
            then(nc.vector.tensor_copy(cum[0:FOX_HEADS], sums))
            nc.vector.tensor_tensor(cum[lo_rows], sums, cum[0:FOX_HEADS].bitcast(F32), ALU.subtract)
            then(nc.vector.tensor_scalar(neg_cum[0:FOX_HEADS], sums, -1.0, None, ALU.mult))
            nc.vector.scalar_tensor_tensor(neg_cum[lo_rows], sums, -1.0, neg_cum[0:FOX_HEADS].bitcast(F32), ALU.mult,
                                           ALU.subtract).then_inc(cum_stored, 1)

        def masks():
            nc.vector.tensor_copy(id_bf[:], ident)
            nc.vector.tensor_copy(neg_bf[:], causal)
            then(nc.vector.memset(cum[:].bitcast(F32), 0.0))
            then(nc.vector.memset(neg_cum[:].bitcast(F32), 0.0))
            dve.wait_ge(picks_landed, 16)
            nc.vector.tensor_copy(pick[:], pick_f32).then_inc(masks_ready, 1)

        def mem_turn(i, l, banks, before):
            dve.wait_ge(mhi_ready, before + 1)
            for c in (2 * i, 2 * i + 1):
                last = nc.vector.scalar_tensor_tensor(
                    m_lo[:, c, :], banks[i % 2][:, (c % 2) * SEQ:(c % 2 + 1) * SEQ], gcols[:, l * KC + c:l * KC + c + 1],
                    m_hi[:, c, :].bitcast(F32), ALU.mult, ALU.subtract)
            last.then_inc(mlo_ready, 1)

        def index(i):
            dve.wait_ge(relu_done, i + 1)
            if i:
                dve.wait_ge(score_done, i)
            for t, c0, w in ((0, 0, 128), (1, 128, 256)):
                r, s = relu_d[:, i % 2, c0:c0 + w], score[:, c0:c0 + w]
                weight = small[:, t, FOX_HEADS + i:FOX_HEADS + i + 1]
                if i == 0:
                    last = nc.vector.tensor_scalar(s, r, weight, None, ALU.mult)
                else:
                    last = nc.vector.scalar_tensor_tensor(s, r, weight, s, ALU.mult, ALU.add)
            last.then_inc(score_done, 1)
            if i == IDX_HEADS - 1:
                dve.wait_ge(score_done, IDX_HEADS)
                nc.vector.tensor_tensor(score[:, 0:128], score[:, 0:128], causal, ALU.add)
                then(nc.vector.tensor_tensor(score[:, 256:384], score[:, 256:384], causal, ALU.add))

        def select(r):
            tiles = (score[:, 0:128], score[:, 128:384])
            nc.vector.max(top8[:, 0, :], tiles[0])
            then(nc.vector.max(top8[:, 1, :], tiles[1]))
            for t in range(T):
                last = nc.vector.match_replace(tiles[t], top8[:, t, :], tiles[t], TAKEN)
            then(last)
            if r == TOPK // 8 - 1:
                nc.vector.tensor_scalar(sel_mask[:], score[:], TAKEN, NEG, ALU.not_equal, ALU.mult).then_inc(sel_ready, 1)

        def heads_step(a, b, c):
            if a is not None:
                dve.wait_ge(s_done, a + 1)
                if a >= 2:
                    dve.wait_ge(exp_done, a - 1)
                for e in range(2):
                    s = PAIRS[a]["s"][e]
                    if PAIRS[a]["kind"] == "mem":
                        last = nc.vector.tensor_reduce(row_max[:, a % 2, 2 * e:2 * e + 2],
                                                       s[:].rearrange("p (t k) -> p t k", t=T), AX.X, ALU.max, negate=True)
                    else:
                        for t, c0, w in qtiles(a):
                            last = nc.vector.tensor_reduce(row_max[:, a % 2, 2 * e + t:2 * e + t + 1],
                                                           s[:, c0:c0 + w], AX.X, ALU.max, negate=True)
                last.then_inc(max_done, 1)
            if c is not None:
                dve.wait_ge(ohi_done, c + 1)
                o = PAIRS[c]["o"]
                nc.vector.tensor_tensor(o_lo[:, o, :], tr[c % 2][:, 0:SEQ], o_hi[:, o, :].bitcast(F32),
                                        ALU.subtract).then_inc(olo_done, 1)

        def normalise(a):
            dve.wait_ge(exp_done, a + 1)
            then(nc.vector.reciprocal(row_inv[:, a % 2, :], row_sum[:, a % 2, :]))
            for e in range(2):
                for t, c0, w in qtiles(a):
                    p = probs[:, a % 2, e, c0:c0 + w]
                    last = nc.vector.tensor_scalar(p, p, row_inv[:, a % 2, 2 * e + t:2 * e + t + 1], None, ALU.mult)
            last.then_inc(prob_done, 1)

        def stage(name, l):
            waiting = None
            for n, item in enumerate(ORDER[name, l]):
                kind, *args = item
                if kind in ("unit", "out") and waiting is not None:
                    normalise(waiting)
                    waiting = None
                if kind == "unit":
                    ahead(args[0]["first"] + args[1])
                elif kind == "take":
                    rotate(*args)
                    forget_gates()
                elif kind == "mean":
                    mean(*args)
                elif kind == "scale":
                    scale(*args)
                elif kind == "rotate":
                    rotate(*args)
                elif kind == "mem_rows":
                    mem_rows()
                    masks()
                    dve.wait_ge(rows_landed, 16)
                    rotation_tables()
                elif kind == "mem_turn":
                    mem_turn(*args, BEFORE[(name, l), n]["quarters"])
                elif kind == "cum":
                    cumulated()
                elif kind == "index":
                    index(*args)
                elif kind == "select":
                    select(*args)
                elif kind == "heads":
                    a, b, c = args
                    if b is not None and waiting == b:
                        normalise(b)
                    heads_step(a, b, c)
                    waiting = a
                elif kind == "out":
                    phase, l, k = args
                    if item != ORDER[name, l][-1]:
                        ahead(start[phase, l] + k)

        lo(0)
        lo(1)
        norm("ffn1", 0)
        for u in range(2, AHEAD):
            lo(u)
        ffn("ffn1", 0)
        for l in range(DEPTH):
            if l:
                norm("ffn1", l)
                ffn("ffn1", l)
            norm("proj", l)
            stage("mix", l)
            residual(NORM["memq", l], start["mixout", l] + KC, 1.0)
            norm("memq", l)
            stage("cross", l)
            residual(NORM["ffn2", l], start["memo", l] + 2, 1.0)
            norm("ffn2", l)
            ffn("ffn2", l)

    @blk.tensor
    def _(pe):
        mm = nc.tensor.matmul

        def split(u, it=0):
            pe.wait_ge(lo_ready, it * ROUND + (u + 1))
            return w_hi[:, u % AHEAD, :], w_lo[:, u % AHEAD, :]

        def products(dst, s_hi, s_lo, m_hi, m_lo, start, stop):
            mm(dst, s_hi, m_hi, start=start, stop=False)
            mm(dst, s_hi, m_lo, start=False, stop=False)
            return mm(dst, s_lo, m_hi, start=False, stop=stop)

        def norm(phase, l):
            n = NORM[phase, l]
            if n == 0:
                pe.wait_ge(tables_landed, 32)
            for g in range(4):
                t = g // 2
                if n == 0:
                    pe.wait_ge(x_landed[t], 16)
                else:
                    pe.wait_ge(h_ready, 4 * (n - 1) + g + 1)
                for c in range(4):
                    k = 4 * (g % 2) + c
                    last = nc.tensor.transpose(turned[g][:, c], h[:, t, k * P:(k + 1) * P], ident)
                last.then_inc(norm_tr, 1)

        def scale_rows(f):
            pe.wait_ge(diag_ready, f + 1)
            mm(tr[0][:, 0:SEQ], tri_ones[:, P:2 * P], diag, start=True, stop=True).then_inc(scale_done, 1)

        def down(u, s_hi, s_lo, first, final, it=0):
            hi, lo = split(u, it)
            for t in range(T):
                a, b = s_hi[:, t * P:(t + 1) * P], s_lo[:, t * P:(t + 1) * P]
                for c in range(2):
                    mm(acc[2 * t + c][:, :], a, hi[:, 512 * c:512 * (c + 1)], start=first, stop=False)
                for c in range(2):
                    mm(acc[2 * t + c][:, :], a, lo[:, 512 * c:512 * (c + 1)], start=False, stop=False)
                for c in range(2):
                    last = mm(acc[2 * t + c][:, :], b, hi[:, 512 * c:512 * (c + 1)], start=False, stop=final)
                if final and t == 0:
                    last.then_inc(tile_summed, 1)
            last.then_inc(unit_used, 1)

        def ffn(phase, l):
            f, u0, n = FFN[phase, l], start[phase, l], NORM[phase, l]

            def chunk(j, u, it=0):
                if j >= 2:
                    pe.wait_ge(ab_ready, it * PER + (FJ * f + j - 1))
                for half in range(2):
                    hi, lo = split(u + half, it)
                    dst = up[j % 2][:, half * SEQ:(half + 1) * SEQ]
                    for k in range(KC):
                        if j == 0 and half == 0 and k % 4 == 0:
                            pe.wait_ge(tlo_ready, 4 * n + 3 + k // 4)
                        last = products(dst, hi[:, k * P:(k + 1) * P], lo[:, k * P:(k + 1) * P], t_hi[:, k, :],
                                        t_lo[:, k, :], k == 0, k == KC - 1)
                    last.then_inc(unit_used, 1)
                    if j == 0 and half == 0:
                        scale_rows(f)

            def out_of(j, u, it=0, first=False, final=False):
                pe.wait_ge(glo_done, it * PER + (FJ * f + j + 1))
                down(u, g_hi[:, j % 2, :], g_lo[:, j % 2, :], first, final, it)

            chunk(0, u0)
            for i in range(PER):
                u = u0 + 2 + 3 * i
                chunk(i + 1, u)
                out_of(i, u + 2, first=i == 0)
            with pe.Fori(1, LOOPS) as it:
                for i in range(PER):
                    u = u0 + 2 + 3 * i
                    pe.wait_ge(ab_ready, it * PER + (FJ * f + i))
                    chunk_in_loop(i + 1, u, it, f)
                    out_of(i, u + 2, it)
            j = FJ - 2
            u = u0 + 2 + 3 * j
            chunk(j + 1, u)
            out_of(j, u + 2)
            out_of(j + 1, u + 3, final=True)

        def chunk_in_loop(j, u, it, f):
            for half in range(2):
                hi, lo = split(u + half, it)
                dst = up[j % 2][:, half * SEQ:(half + 1) * SEQ]
                for k in range(KC):
                    last = products(dst, hi[:, k * P:(k + 1) * P], lo[:, k * P:(k + 1) * P], t_hi[:, k, :],
                                    t_lo[:, k, :], k == 0, k == KC - 1)
                last.then_inc(unit_used, 1)

        def tile_unit(b, i, t):
            s_hi, s_lo = (m_hi, m_lo) if b["name"] == "memkv" else (t_hi, t_lo)
            per, w = KC // b["n_units"], b["ncols"]
            hi, lo = split(b["first"] + i)
            if b["name"] == "memkv":
                pe.wait_ge(mlo_ready, 4 * (b["l"] + 1))
            elif b["before"] is None:
                n = NORM["memq" if b["name"] == "memq" else "proj", b["l"]]
                pe.wait_ge(tlo_ready, 4 * n + 2 * t + (per * (i + 1) - 1) // 4 + 1)
            if i == 0 and b["before"] is not None:
                pe.wait_ge(tile_taken, T * b["before"] + t + 1)
            dst = acc[b["bank"] + t][:, 0:w]
            for kk in range(per):
                k = per * i + kk
                last = products(dst, s_hi[:, k, t * P:(t + 1) * P], s_lo[:, k, t * P:(t + 1) * P],
                                hi[:, kk * w:(kk + 1) * w], lo[:, kk * w:(kk + 1) * w], k == 0, k == KC - 1)
            if t == 0 and i == b["n_units"] - 1:
                last.then_inc(tile_done, 1)
            if t == T - 1:
                last.then_inc(unit_used, 1)

        def block_unit(b, i):
            if b["name"] not in ("iq", "q0", "memq") or i >= 2:
                for t in range(T):
                    tile_unit(b, i, t)
            elif i == 0:
                for t in range(T):
                    tile_unit(b, 0, t)
                    tile_unit(b, 1, t)

        def turn(b, before):
            pe.wait_ge(heads_ready, b["q"] + 1)
            if b["q"]:
                pe.wait_ge(heads_stored, b["q"])
            if before["pv"]:
                pe.wait_ge(olo_done, before["pv"])
            for pair in range(b["nh"] // 2):
                for t in range(T):
                    at = (pair % 2) * SEQ + t * P
                    last = nc.tensor.transpose(tr[pair // 2][:, at:at + P], heads_raw[:, t, pair * P:(pair + 1) * P], ident)
            last.then_inc(heads_tr, 1)

        def mem_turn(i, l, banks, before):
            if before == 0:
                pe.wait_ge(scaled_act, 1)
                pe.wait_ge(scaled_dve, 1)
            if i >= 2:
                pe.wait_ge(mlo_ready, before - 1)
            for c in (2 * i, 2 * i + 1):
                for t in range(T):
                    at = (c % 2) * SEQ + t * P
                    last = nc.tensor.transpose(banks[i % 2][:, at:at + P], memh[:, t, c * P:(c + 1) * P], ident)
            last.then_inc(mem_tr, 1)

        def cumulate():
            pe.wait_ge(log_ready, 1)
            pe.wait_ge(mlo_ready, 4)
            dst = up[0][0:FOX_HEADS, :]
            mm(dst[:, 0:SEQ], forget[:, 5, 0], tri_ones, start=True, stop=False)
            mm(dst[:, P:SEQ], forget[:, 5, 1], tri_ones[:, 0:P], start=False, stop=True).then_inc(cum_done, 1)

        def index(i):
            if i == 0:
                pe.wait_ge(heads_stored, BLOCK["small", 0]["q"] + 1)
                pe.wait_ge(tile_taken, T * (BLOCK["small", 0]["i"] + 1))
            if i >= 2:
                pe.wait_ge(relu_done, i - 1)
            e = slice(HD * (i % 2), HD * (i % 2 + 1))
            for t, c0, w in ((0, 0, 128), (1, 128, 256)):
                last = mm(acc[2 + i % 2][:, c0:c0 + w], idx_t[e, i // 2, t * P:(t + 1) * P], idx_t[e, 4, 0:w],
                          start=True, stop=True)
            last.then_inc(dots_done, 1)

        def scores(a, before):
            pair, kind = PAIRS[a], PAIRS[a]["kind"]
            pe.wait_ge(heads_stored, before["turns"])
            if a and pair["s"][0] is acc[2]:
                pe.wait_ge(exp_done, a)
            if a == 0:
                pe.wait_ge(relu_done, IDX_HEADS)
                pe.wait_ge(masks_ready, 1)
            if kind == "dsa":
                pe.wait_ge(sel_ready, 1)
            if kind == "fox":
                pe.wait_ge(cum_stored, 1)
            if kind == "mem":
                pe.wait_ge(mlo_ready, before["quarters"])
            for e in range(2):
                rows = slice(HD * e, HD * (e + 1))
                for t, c0, w in qtiles(a):
                    s = pair["s"][e]
                    dst, diag = s[:, c0:c0 + w], s[:, c0 + w - P:c0 + w]
                    last = mm(dst, pair["q"][rows, t * P:(t + 1) * P], pair["k"][rows, 0:w], start=True,
                              stop=kind == "mem")
                    if kind == "mem":
                        continue
                    if kind == "fox":
                        mine = pair["head"] + e
                        mm(dst, cum[:, t * P:(t + 1) * P], pick[:, mine, 0:w], start=False, stop=False)
                        mm(dst, pick[:, mine, 0:P], neg_cum[:, 0:w], start=False, stop=False)
                    if kind == "dsa":
                        mm(dst, id_bf[:], sel_mask[:, c0:c0 + w], start=False, stop=False)
                    last = mm(diag, id_bf[:], neg_bf[:], start=False, stop=True)
            last.then_inc(s_done, 1)

        def heads(a, b, c, before):
            if a is not None:
                scores(a, before)
            if b is not None:
                pe.wait_ge(prob_done, b + 1)
                if b:
                    pe.wait_ge(pt_stored, b)
                turns = [(0, 0), (128, 128), (256, 256)]
                if PAIRS[b]["kind"] == "mem":
                    turns = [(0, 0), (256, 128), (128, 256), (384, 384)]
                for e in range(2):
                    for src, dst in turns:
                        last = nc.tensor.transpose(up[e][:, dst:dst + P], probs[:, b % 2, e, src:src + P], ident)
                last.then_inc(ptr_done, 1)
            if c is not None:
                pe.wait_ge(pt_stored, c + 1)
                pe.wait_ge(tile_taken, T * (values_of(c) + 1))
                pe.wait_ge(heads_stored, before["turns"])
                if c >= 2:
                    pe.wait_ge(olo_done, c - 1)
                v, late = PAIRS[c]["v"], SEQ - (cols(c) - SEQ)
                for e in range(2):
                    rows = slice(HD * e, HD * (e + 1))
                    mm(tr[c % 2][rows, 0:SEQ], v[:, 0, rows], probs_t[:, c % 2, e, 0:SEQ], start=True, stop=False)
                    last = mm(tr[c % 2][rows, late:SEQ], v[:, 1, rows], probs_t[:, c % 2, e, SEQ:cols(c)],
                              start=False, stop=True)
                last.then_inc(pv_done, 1)

        def values_of(c):
            kind, o = PAIRS[c]["kind"], PAIRS[c]["o"]
            l = 0 if c < pairs_in["moba", 1][0] else 1
            name = {"dsa": "dv", "fox": "fv", "mem": "memkv", "moba": "v0" if o < 4 else "v1"}[kind]
            return BLOCK[name, l]["i"]

        def out_unit(phase, l, k):
            first = pairs_in[("fox" if l == 0 else "moba") if phase == "mixout" else "mem", l][0]
            pe.wait_ge(olo_done, first + k + 1)
            if k == 0 and phase == "mixout":
                pe.wait_ge(tile_taken, T * (BLOCK["memkv", l]["i"] + 1))
                pe.wait_ge(exp_done, pairs_in["mem", l][0])
            down(start[phase, l] + k, o_hi[:, k, :], o_lo[:, k, :], k == 0, k == (KC if phase == "mixout" else 2) - 1)

        def stage(name, l):
            for n, item in enumerate(ORDER[name, l]):
                kind, *args = item
                before = BEFORE[(name, l), n]
                if kind == "unit":
                    block_unit(*args)
                elif kind == "turn":
                    turn(*args, before)
                elif kind == "mem_turn":
                    mem_turn(*args, before["quarters"])
                elif kind == "cum":
                    cumulate()
                elif kind == "index":
                    index(*args)
                elif kind == "heads":
                    heads(*args, before)
                elif kind == "out":
                    out_unit(*args)

        for l in range(DEPTH):
            norm("ffn1", l)
            ffn("ffn1", l)
            norm("proj", l)
            stage("mix", l)
            norm("memq", l)
            stage("cross", l)
            norm("ffn2", l)
            ffn("ffn2", l)

    ctx.close()


def lay_out(a):
    def rows(w):
        return w.reshape(KC, P, -1).transpose(1, 0, 2)

    def ffn(which, l):
        w_in, w_out = a[which + "_w_in"][l], a[which + "_w_out"][l]
        up = w_in.reshape(KC, P, 2, FJ, P).transpose(2, 3, 1, 0, 4).reshape(2, FJ, P, UNIT)
        down = w_out.reshape(FJ, P, UNIT)
        return {which + "a": up[0], which + "b": up[1], which + "o": down}

    made = {}
    for l in range(DEPTH):
        for which in ("ffn1", "ffn2"):
            for name, w in ffn(which, l).items():
                made[name, l] = w
        made["memkv", l] = rows(a["mem_wkv"][l]).reshape(P, 4, UNIT).transpose(1, 0, 2)
        made["memq", l] = rows(a["mem_wq"][l]).reshape(P, 2, UNIT).transpose(1, 0, 2)
        made["memo", l] = a["mem_wo"][l].reshape(2, P, UNIT)
        made["mixout", l] = a["mix_w_out"][l].reshape(KC, P, UNIT)
        w = a["even_w_in"][0] if l == 0 else a["odd_w_in"][0]
        for name, c0 in blocks_of(l):
            if name == "small":
                f0, i0 = 3 * FOX_HEADS * HD, w.shape[1] - HD - IDX_HEADS
                part = rows(np.concatenate([w[:, i0:i0 + HD], w[:, f0:f0 + FOX_HEADS], w[:, i0 + HD:]], axis=1))
                flat = np.ascontiguousarray(part).reshape(P, KC * SMALL)
                made["small", l] = np.concatenate([flat, np.zeros((P, UNIT - KC * SMALL), w.dtype)], axis=1)[None]
            else:
                made["mix:" + name, l] = rows(w[:, c0:c0 + 512]).reshape(P, 4, UNIT).transpose(1, 0, 2)
    units, _ = unit_list()
    stream = np.stack([made[name, l][i] for name, l, i in units])

    norms = [a["mem_norm_m"][0], a["mem_norm_m"][1]]
    for l in range(DEPTH):
        norms += [a["ffn1_norm"][l], a["mix_norm"][l], a["mem_norm_x"][l], a["ffn2_norm"][l]]
    heads = {"mem_q0": a["mem_q_norm"][0], "mem_k0": a["mem_k_norm"][0], "mem_q1": a["mem_q_norm"][1],
             "mem_k1": a["mem_k_norm"][1]}
    for kind in ("fox", "dsa", "moba"):
        for part in ("q", "k"):
            heads[f"{kind}_{part}"] = a[f"{kind}_{part}_norm"][0]
    head_cols = []
    for name in HEAD_GAINS:
        g = heads[name]
        if name in ROTATED:
            g = np.concatenate([np.ones(ROT, g.dtype), g[ROT:]])
        head_cols.append(np.concatenate([g, g])[:, None])
    gain_cols = np.concatenate([g.reshape(KC, P).transpose(1, 0) for g in norms] + head_cols, axis=1)
    gain_rows = np.concatenate([heads[name][0:ROT] for name in ROTATED] + [a["even_b_forget"][0]])[None]

    f32 = np.float32
    i = np.arange(P)
    pos = np.arange(SEQ, dtype=f32)
    inv = f32(500000.0) ** (-np.arange(0, ROT, 2, dtype=f32) / f32(ROT))
    ang = (pos[:, None] * inv[None, :]).astype(f32)
    consts = np.zeros((P, C_END), f32)
    consts[:, C_ID:C_ID + P] = np.eye(P)
    consts[:, C_TRI:C_TRI + P] = i[:, None] <= i[None, :]
    consts[:, C_ONE:C_ONE + P] = 1.0
    consts[:, C_NEG:C_NEG + P] = np.where(i[None, :] > i[:, None], NEG, 0.0)
    consts[:, C_COS:C_COS + 16] = np.cos(ang).reshape(T, P, 8).transpose(1, 0, 2).reshape(P, 16)
    consts[:, C_SIN:C_SIN + 16] = np.sin(ang).reshape(T, P, 8).transpose(1, 0, 2).reshape(P, 16)
    consts[:, C_HALF:] = -0.5
    picks = np.zeros((CUM_ROWS, FOX_HEADS, SEQ), f32)
    for i in range(FOX_HEADS):
        picks[[i, CUM_LO + i], i] = 1.0
    return {"x": a["x"], "mem": a["mem"], "stream": stream, "gain_cols": gain_cols, "gain_rows": gain_rows,
            "consts": consts, "picks": picks.reshape(CUM_ROWS, -1)}


def kernel(**inputs):
    import numpy as _np
    import concourse.bacc as _bacc
    from concourse import mybir as _mybir
    from concourse.bass_utils import run_bass_kernel_spmd as _run

    a = {k: _np.asarray(v) for k, v in inputs.items()}
    nc = _bacc.Bacc("TRN2", target_bir_lowering=False, num_devices=1)
    arrays, args = {}, []
    for name, v in lay_out(a).items():
        v = _np.ascontiguousarray(v)
        arrays[f"in_{name}_dram"] = v
        args.append(nc.dram_tensor(f"in_{name}_dram", v.shape, _mybir.dt.from_np(v.dtype), kind="ExternalInput").ap())
    args.append(nc.dram_tensor("out_0_dram", (1, SEQ, D), F32, kind="ExternalOutput").ap())
    build(nc, *args)
    r = _run(nc, [arrays], core_ids=[0])
    return r.results[0]["out_0_dram"]
```
